# Optimizing a Trainium2 kernel written in Bass

```python
import jax, jax.numpy as jnp
from jax import lax
import numpy as np

D_MODEL = 1024
BATCH = 1
SEQ = 256
DEPTH = 2

BLOCK = 128
EPS = 1e-6
ROPE_BASE = 10000.0
MLA_HEADS = 8
MLA_NOPE = 64
MLA_ROPE = 32
MLA_V = 64
MLA_Q_RANK = 384
MLA_KV_RANK = 256
RET_HEADS = 8
RET_DK = 64
RET_DV = 128
SWA_HEADS = 16
SWA_KV_HEADS = 2
SWA_DIM = 64
WINDOW = 128
SB_HEADS = 8
SB_DIM = 64
D_FF = 3584
N_EXPERTS = 8
TOP_K = 2
MOE_BLOCK = 256

AB_SPLITS = (MLA_Q_RANK, MLA_KV_RANK, MLA_ROPE, RET_HEADS * RET_DK, RET_HEADS * RET_DK, RET_HEADS * RET_DV, RET_HEADS * RET_DV)
AB_IN = sum(AB_SPLITS)
AB_MIX = MLA_HEADS * MLA_V + RET_HEADS * RET_DV
CD_SPLITS = (SWA_HEADS * SWA_DIM, SWA_KV_HEADS * SWA_DIM, SWA_KV_HEADS * SWA_DIM, SB_HEADS * SB_DIM, SB_HEADS * SB_DIM, SB_HEADS * SB_DIM)
CD_IN = sum(CD_SPLITS)
CD_MIX = SWA_HEADS * SWA_DIM + SB_HEADS * SB_DIM

kernel_name = "hybrid_mla_retention_swa_stickbreak_moe"

def _split(x, sizes):
    return jnp.split(x, [int(i) for i in np.cumsum(sizes)[:-1]], axis=-1)

def _rmsnorm(x, g):
    xf = x.astype(jnp.float32)
    y = xf * lax.rsqrt(jnp.mean(xf * xf, axis=-1, keepdims=True) + EPS)
    return (y * g.astype(jnp.float32)).astype(x.dtype)

def _rope(x, pos):
    half = x.shape[-1] // 2
    inv_freq = ROPE_BASE ** (-jnp.arange(half, dtype=jnp.float32) / half)
    ang = pos.astype(jnp.float32)[:, None] * inv_freq[None, :]
    cos = jnp.cos(ang)[:, None, :]
    sin = jnp.sin(ang)[:, None, :]
    xf = x.astype(jnp.float32)
    x1, x2 = xf[..., :half], xf[..., half:]
    return jnp.concatenate([x1 * cos - x2 * sin, x1 * sin + x2 * cos], axis=-1).astype(x.dtype)

def _to_blocks(t):
    B, S = t.shape[:2]
    return jnp.moveaxis(t.reshape((B, S // BLOCK, BLOCK) + t.shape[2:]), 1, 0)

def _from_blocks(t):
    t = jnp.moveaxis(t, 0, 1)
    return t.reshape((t.shape[0], t.shape[1] * t.shape[2]) + t.shape[3:])

def _causal_softmax_attention(q, k, v):
    S = q.shape[1]
    scale = q.shape[-1] ** -0.5
    kpos = jnp.arange(S)

    def block(args):
        qi, i = args
        s = jnp.einsum('bqhd,bkhd->bhqk', qi, k, preferred_element_type=jnp.float32) * scale
        qpos = i * BLOCK + jnp.arange(BLOCK)
        s = jnp.where(kpos[None, :] <= qpos[:, None], s, -jnp.inf)
        p = jax.nn.softmax(s, axis=-1)
        return jnp.einsum('bhqk,bkhd->bqhd', p.astype(v.dtype), v)

    return _from_blocks(lax.map(block, (_to_blocks(q), jnp.arange(S // BLOCK))))

def _retention(q, k, v):
    B, S, H, dk = q.shape
    dv = v.shape[-1]
    log_gamma = jnp.log1p(-(2.0 ** (-5.0 - jnp.arange(H, dtype=jnp.float32))))
    idx = jnp.arange(BLOCK, dtype=jnp.float32)
    rel = idx[:, None] - idx[None, :]
    decay_in = jnp.where(rel >= 0, jnp.exp(log_gamma[:, None, None] * jnp.maximum(rel, 0.0)), 0.0)
    q_decay = jnp.exp(log_gamma[:, None] * (idx + 1.0))
    k_decay = jnp.exp(log_gamma[:, None] * (BLOCK - 1.0 - idx))
    chunk_decay = jnp.exp(log_gamma * BLOCK)
    qc = _to_blocks(q.astype(jnp.float32))
    kc = _to_blocks(k.astype(jnp.float32)) * (dk ** -0.5)
    vc = _to_blocks(v.astype(jnp.float32))
    inner = jnp.einsum('nbqhd,nbkhd->nbhqk', qc, kc) * decay_in[None, None]
    out_inner = jnp.einsum('nbhqk,nbkhv->nbqhv', inner, vc)
    kv_chunk = jnp.einsum('nbkhd,hk,nbkhv->nbhdv', kc, k_decay, vc)

    def step(state, kv):
        return state * chunk_decay[None, :, None, None] + kv, state

    _, prev = lax.scan(step, jnp.zeros((B, H, dk, dv), jnp.float32), kv_chunk)
    out_cross = jnp.einsum('nbqhd,hq,nbhdv->nbqhv', qc, q_decay, prev)
    return _from_blocks(out_inner + out_cross)

def _head_groupnorm(y, g):
    B, S, H, dv = y.shape
    mu = jnp.mean(y, axis=-1, keepdims=True)
    var = jnp.mean(jnp.square(y - mu), axis=-1, keepdims=True)
    yn = (y - mu) * lax.rsqrt(var + EPS)
    return yn.reshape(B, S, H * dv) * g.astype(jnp.float32)

def _mixer_mla_retention(h, w_in, q_norm, w_uq, kv_norm, w_ukv, ret_gn, w_out):
    B, S, _ = h.shape
    pos = jnp.arange(S)
    q_lat, kv_lat, k_rope, rq, rk, rv, rg = _split(h @ w_in, AB_SPLITS)
    qh = (_rmsnorm(q_lat, q_norm) @ w_uq).reshape(B, S, MLA_HEADS, MLA_NOPE + MLA_ROPE)
    kvh = (_rmsnorm(kv_lat, kv_norm) @ w_ukv).reshape(B, S, MLA_HEADS, MLA_NOPE + MLA_V)
    q = jnp.concatenate([qh[..., :MLA_NOPE], _rope(qh[..., MLA_NOPE:], pos)], axis=-1)
    k_pe = jnp.broadcast_to(_rope(k_rope[:, :, None, :], pos), (B, S, MLA_HEADS, MLA_ROPE))
    k = jnp.concatenate([kvh[..., :MLA_NOPE], k_pe], axis=-1)
    mla = _causal_softmax_attention(q, k, kvh[..., MLA_NOPE:]).reshape(B, S, MLA_HEADS * MLA_V)
    ret = _retention(_rope(rq.reshape(B, S, RET_HEADS, RET_DK), pos),
                     _rope(rk.reshape(B, S, RET_HEADS, RET_DK), pos),
                     rv.reshape(B, S, RET_HEADS, RET_DV))
    ret = jax.nn.silu(rg.astype(jnp.float32)) * _head_groupnorm(ret, ret_gn)
    mixed = jnp.concatenate([mla, ret.astype(h.dtype)], axis=-1)
    return mixed @ w_out

def _alibi_slopes(n):
    return 2.0 ** (-8.0 * jnp.arange(1, n + 1, dtype=jnp.float32) / n)

def _sliding_window_sink_attention(q, k, v, sinks):
    B, S, HQ, d = q.shape
    HKV = k.shape[2]
    G = HQ // HKV
    nb = S // WINDOW
    scale = d ** -0.5

    def band(t):
        tb = t.reshape(B, nb, WINDOW, HKV, d)
        prev = jnp.pad(tb, ((0, 0), (1, 0), (0, 0), (0, 0), (0, 0)))[:, :-1]
        return jnp.moveaxis(jnp.concatenate([prev, tb], axis=2), 1, 0)

    qb = jnp.moveaxis(q.reshape(B, nb, WINDOW, HKV, G, d), 1, 0)
    slopes = _alibi_slopes(HQ).reshape(HKV, G)[:, :, None, None]
    sink = sinks.astype(jnp.float32).reshape(HKV, G)[None, :, :, None, None]
    dist = jnp.arange(WINDOW)[:, None] + WINDOW - jnp.arange(2 * WINDOW)[None, :]
    in_window = (dist >= 0) & (dist < WINDOW)
    dist_f = dist.astype(jnp.float32)

    def block(args):
        qi, ki, vi, i = args
        s = jnp.einsum('bqhgd,bkhd->bhgqk', qi, ki, preferred_element_type=jnp.float32) * scale - slopes * dist_f
        valid = in_window & (((i - 1) * WINDOW + jnp.arange(2 * WINDOW)) >= 0)[None, :]
        s = jnp.where(valid, s, -jnp.inf)
        m = jnp.maximum(jnp.max(s, axis=-1, keepdims=True), sink)
        p = jnp.exp(s - m)
        p = p / (jnp.sum(p, axis=-1, keepdims=True) + jnp.exp(sink - m))
        return jnp.einsum('bhgqk,bkhd->bqhgd', p.astype(vi.dtype), vi)

    out = lax.map(block, (qb, band(k), band(v), jnp.arange(nb)))
    return jnp.moveaxis(out, 0, 1).reshape(B, S, HQ * d)

def _stick_breaking_attention(q, k, v):
    S = q.shape[1]
    scale = q.shape[-1] ** -0.5
    kpos = jnp.arange(S)

    def block(args):
        qi, i = args
        z = jnp.einsum('bqhd,bkhd->bhqk', qi, k, preferred_element_type=jnp.float32) * scale
        qpos = i * BLOCK + jnp.arange(BLOCK)
        before = kpos[None, :] < qpos[:, None]
        log_keep = jnp.where(before, jax.nn.log_sigmoid(-z), 0.0)
        log_after = lax.cumsum(log_keep, axis=3, reverse=True) - log_keep
        a = jnp.where(before, jnp.exp(jax.nn.log_sigmoid(z) + log_after), 0.0)
        return jnp.einsum('bhqk,bkhd->bqhd', a.astype(v.dtype), v)

    return _from_blocks(lax.map(block, (_to_blocks(q), jnp.arange(S // BLOCK))))

def _mixer_swa_stickbreak(h, w_in, sinks, w_out):
    B, S, _ = h.shape
    sq, sk, sv, bq, bk, bv = _split(h @ w_in, CD_SPLITS)
    swa = _sliding_window_sink_attention(sq.reshape(B, S, SWA_HEADS, SWA_DIM),
                                         sk.reshape(B, S, SWA_KV_HEADS, SWA_DIM),
                                         sv.reshape(B, S, SWA_KV_HEADS, SWA_DIM), sinks)
    sb = _stick_breaking_attention(bq.reshape(B, S, SB_HEADS, SB_DIM),
                                   bk.reshape(B, S, SB_HEADS, SB_DIM),
                                   bv.reshape(B, S, SB_HEADS, SB_DIM)).reshape(B, S, SB_HEADS * SB_DIM)
    return jnp.concatenate([swa, sb], axis=-1) @ w_out

def _swiglu(h, w_gate, w_up, w_down):
    return (jax.nn.silu(h @ w_gate) * (h @ w_up)) @ w_down

def _moe(h, router, w_gate, w_up, w_down):
    B, S, D = h.shape
    T = B * S
    TK = T * TOP_K
    xf = h.reshape(T, D)
    logits = (xf @ router).astype(jnp.float32)
    top_logits, top_idx = lax.top_k(logits, TOP_K)
    gates = jax.nn.softmax(top_logits, axis=-1)
    expert = top_idx.reshape(-1).astype(jnp.int32)
    token = jnp.repeat(jnp.arange(T, dtype=jnp.int32), TOP_K)
    gate = gates.reshape(-1)
    order = jnp.argsort(expert)
    se, st, sg = expert[order], token[order], gate[order]
    counts = jnp.zeros((N_EXPERTS,), jnp.int32).at[expert].add(1)
    padded = ((counts + MOE_BLOCK - 1) // MOE_BLOCK) * MOE_BLOCK
    pad_end = jnp.cumsum(padded)
    pad_start = pad_end - padded
    grp_start = jnp.cumsum(counts) - counts
    dest = pad_start[se] + (jnp.arange(TK, dtype=jnp.int32) - grp_start[se])
    cap = -(-TK // MOE_BLOCK) * MOE_BLOCK + N_EXPERTS * MOE_BLOCK
    nblk = cap // MOE_BLOCK
    buf_tok = jnp.zeros((cap,), jnp.int32).at[dest].set(st)
    buf_gate = jnp.zeros((cap,), jnp.float32).at[dest].set(sg)
    blk_start = jnp.arange(nblk, dtype=jnp.int32) * MOE_BLOCK
    blk_exp = jnp.minimum(jnp.searchsorted(pad_end, blk_start, side='right'), N_EXPERTS - 1)
    xg = xf[buf_tok].reshape(nblk, MOE_BLOCK, D)

    def expert_block(args):
        xb, e = args
        return (jax.nn.silu(xb @ w_gate[e]) * (xb @ w_up[e])) @ w_down[e]

    yg = lax.map(expert_block, (xg, blk_exp)).reshape(cap, D)
    out = jnp.zeros((T, D), h.dtype).at[buf_tok].add((yg * buf_gate[:, None]).astype(h.dtype))
    return out.reshape(B, S, D)

def setup_inputs(seed: int = 0) -> dict:
    key = jax.random.key(seed)
    ks = iter(jax.random.split(key, 32))
    NE = (DEPTH + 1) // 2
    NO = DEPTH // 2

    def w(shape, fan_in):
        return jax.random.normal(next(ks), shape, jnp.float32) * (fan_in ** -0.5)

    def gain(shape):
        return 1.0 + 0.02 * jax.random.normal(next(ks), shape, jnp.float32)

    return {
        'x': jax.random.normal(next(ks), (BATCH, SEQ, D_MODEL), jnp.float32),
        'ab_norm': gain((NE, D_MODEL)),
        'ab_w_in': w((NE, D_MODEL, AB_IN), D_MODEL),
        'mla_q_norm': gain((NE, MLA_Q_RANK)),
        'mla_w_uq': w((NE, MLA_Q_RANK, MLA_HEADS * (MLA_NOPE + MLA_ROPE)), MLA_Q_RANK),
        'mla_kv_norm': gain((NE, MLA_KV_RANK)),
        'mla_w_ukv': w((NE, MLA_KV_RANK, MLA_HEADS * (MLA_NOPE + MLA_V)), MLA_KV_RANK),
        'ret_gn': gain((NE, RET_HEADS * RET_DV)),
        'ab_w_out': w((NE, AB_MIX, D_MODEL), AB_MIX),
        'ffn_norm': gain((NE, D_MODEL)),
        'ffn_w_gate': w((NE, D_MODEL, D_FF), D_MODEL),
        'ffn_w_up': w((NE, D_MODEL, D_FF), D_MODEL),
        'ffn_w_down': w((NE, D_FF, D_MODEL), D_FF),
        'cd_norm': gain((NO, D_MODEL)),
        'cd_w_in': w((NO, D_MODEL, CD_IN), D_MODEL),
        'swa_sinks': 0.5 * jax.random.normal(next(ks), (NO, SWA_HEADS), jnp.float32),
        'cd_w_out': w((NO, CD_MIX, D_MODEL), CD_MIX),
        'moe_norm': gain((NO, D_MODEL)),
        'moe_router': w((NO, D_MODEL, N_EXPERTS), D_MODEL),
        'moe_w_gate': w((NO, N_EXPERTS, D_MODEL, D_FF), D_MODEL),
        'moe_w_up': w((NO, N_EXPERTS, D_MODEL, D_FF), D_MODEL),
        'moe_w_down': w((NO, N_EXPERTS, D_FF, D_MODEL), D_FF),
        'final_norm': gain((D_MODEL,)),
    }

def reference(x, ab_norm, ab_w_in, mla_q_norm, mla_w_uq, mla_kv_norm, mla_w_ukv, ret_gn, ab_w_out,
              ffn_norm, ffn_w_gate, ffn_w_up, ffn_w_down, cd_norm, cd_w_in, swa_sinks, cd_w_out,
              moe_norm, moe_router, moe_w_gate, moe_w_up, moe_w_down, final_norm):
    h = x
    for layer in range(DEPTH):
        i = layer // 2
        if layer % 2 == 0:
            h = h + _mixer_mla_retention(_rmsnorm(h, ab_norm[i]), ab_w_in[i], mla_q_norm[i], mla_w_uq[i],
                                         mla_kv_norm[i], mla_w_ukv[i], ret_gn[i], ab_w_out[i])
            h = h + _swiglu(_rmsnorm(h, ffn_norm[i]), ffn_w_gate[i], ffn_w_up[i], ffn_w_down[i])
        else:
            h = h + _mixer_swa_stickbreak(_rmsnorm(h, cd_norm[i]), cd_w_in[i], swa_sinks[i], cd_w_out[i])
            h = h + _moe(_rmsnorm(h, moe_norm[i]), moe_router[i], moe_w_gate[i], moe_w_up[i], moe_w_down[i])
    return _rmsnorm(h, final_norm)


_drawn_inputs = setup_inputs


def setup_inputs(seed=0):
    import zlib

    import numpy as np

    out = dict(_drawn_inputs(seed))
    spreads = {}
    factors = {'mla_q_norm': 8.0,
     'mla_kv_norm': 3.275,
     'ret_gn': 3.955,
     'cd_norm': 3.147,
     'swa_sinks': 26.665,
     'final_norm': 7.989,
     'ffn_norm': 3.0,
     'moe_norm': 4.513}
    for name, (base, spread) in spreads.items():
        noise = np.random.default_rng([zlib.crc32(name.encode()), seed]).standard_normal(out[name].shape)
        drawn = base * np.exp(spread * noise) if base else spread * noise
        out[name] = __import__('jax').numpy.asarray(drawn.astype(out[name].dtype))
    for name, factor in factors.items():
        out[name] = (out[name] * factor).astype(out[name].dtype)
    return out
```

```python
from contextlib import ExitStack

import concourse.bass as bass
from concourse import mybir

F32 = mybir.dt.float32
F32R = mybir.dt.float32r
I32 = mybir.dt.int32
ALU = mybir.AluOpType
ACT = mybir.ActivationFunctionType
AX = mybir.AxisListType.X

P = 128
TB = 2
D = 1024
KD = D // P
EPS = 1e-6
MASKED = -1e30

Q_RANK, KV_RANK, ROPE = 384, 256, 32
RET_H, RET_DK, RET_DV = 8, 64, 128
AB_IN = 3744
A_KV, A_KR, A_RQK, A_RV, A_RG = 384, 640, 672, 1696, 2720
MLA_H, MLA_D, NOPE = 8, 96, 64
CD_IN = 2816
SWA_H, SWA_KV, HD = 16, 2, 64
C_SK, C_SV, C_BQ, C_BK, C_BV = 1024, 1152, 1280, 1792, 2304
SB_H = 8
MIX = 1536
KM = MIX // P
FF = 3584
FC = 512
NFC = FF // FC
NE = 8
CAP = 128

IN_CH = 8
UNIT = 1024
NBUF = 4
SLOT = 2048
SLOT_BYTES = SLOT * 4

U_AB_IN = 0
U_AB_OUT = U_AB_IN + 4 * IN_CH
U_FFN = U_AB_OUT + KM
U_CD_IN = U_FFN + 12 * NFC
U_CD_OUT = U_CD_IN + 4 * IN_CH
U_MOE = U_CD_OUT + KM
MOE_SLOTS = 14
DOWN_SPLIT = tuple(range(7))


def moe_items():
    items = [("g", 0), ("u", 0)]
    for c in range(1, NFC):
        items += [("g", c), ("u", c), ("d", c - 1)]
    return items + [("d", NFC - 1)]


def moe_plan():
    plan, units, plain = [], 0, 0
    for kind, c in moe_items():
        for half in range(2):
            if kind != "d" or c in DOWN_SPLIT:
                units += 2
                plan.append((kind, c, half, "split", units))
            else:
                plain += 1
                plan.append((kind, c, half, "plain", plain))
    return plan, units, plain


CONST_WIDTHS = dict(
    ident=128, incl=128, negones=128, ones=128, before=128, strict=128, iota=256, cos_m=64, sin_m=64,
    cos_r=128, sin_r=128, causal=384, dist=384, sb_neg=384, lower8=64, g_ab=8, g_lat=5, g_mix=12,
    g_ffn=8, g_cd=8, g_one=12, g_moe=8, sinks=16, eps=1)
CONST_AT, _at = {}, 0
for _name, _w in CONST_WIDTHS.items():
    CONST_AT[_name] = _at
    _at += _w
NCONST = _at


def trunk(nc, x, consts, decay_t, ab_w_in, w_uq, w_ukv, ab_w_out, f_gate, f_up, f_down,
          cd_w_in, cd_w_out, router, m_gate, m_up, m_down, final_gain, out):
    plan, UPE, PPE = moe_plan()
    with ExitStack() as ctx:
        base = 16640

        def place(name, shape, dt=F32, at=None):
            return nc.alloc_sbuf_tensor_at(name, shape, dt, offset=base + at)[tuple(slice(None) for _ in shape)]

        H_AT, XN_AT, XT_AT, SPLIT_AT = 0, 8192, 16384, 32768
        RING_AT = SPLIT_AT + 32768
        CONST_BYTES = 4 * NCONST
        CONST_OFF = RING_AT + 7 * SLOT_BYTES
        ARENA = CONST_OFF + (CONST_BYTES + 63) // 64 * 64 + 1024
        SMALL = ARENA - 1024
        RINGB_AT = (229344 - base - 7 * SLOT_BYTES) // 64 * 64
        assert RINGB_AT >= ARENA + 19968, (RINGB_AT, ARENA)

        h = place("h", [P, TB, D], at=H_AT)
        xn = place("xn", [P, TB, D], at=XN_AT)
        xT_hi = place("xT_hi", [P, KD, 256], F32R, at=XT_AT)
        xT_lo = place("xT_lo", [P, KD, 256], F32R, at=XT_AT + 8192)
        xT32 = place("xT32", [P, KD, 256], at=XT_AT)
        w_hi = place("w_hi", [P, NBUF, UNIT], F32R, at=SPLIT_AT)
        w_lo = place("w_lo", [P, NBUF, UNIT], F32R, at=SPLIT_AT + 16384)
        ring = [place(f"ring{s}", [P, SLOT], at=RING_AT + s * SLOT_BYTES) for s in range(7)]
        ring += [place(f"ring{s + 7}", [P, SLOT], at=RINGB_AT + s * SLOT_BYTES) for s in range(7)]
        cst = place("cst", [P, NCONST], at=CONST_OFF)
        small = place("small", [P, 256], at=SMALL)

        def const(name, a=0, b=None):
            o = CONST_AT[name]
            return cst[:, o + a:o + (CONST_WIDTHS[name] if b is None else b)]

        qT = place("qT", [P, MLA_H, 256], at=ARENA)
        kT = place("kT", [P, MLA_H, 256], at=ARENA + 8192)
        rT = place("rT", [P, 8, 256], at=ARENA + 16384)
        proj = place("proj", [P, TB, AB_IN], at=ARENA + 24576)
        mix = place("mix", [P, TB, MIX], at=ARENA + 54528)
        latT = place("latT", [P, 5, 256], at=ARENA + 66816)
        rope_t = place("rope_t", [P, 1024], at=ARENA + 71936)
        gn_t = place("gn_t", [P, 256], at=ARENA + 76032)
        assert ARENA + 77056 <= 229344 - base
        decay = place("decay", [P, RET_H, 256], at=XT_AT)
        rqk = place("rqk", [P, TB, 1024], at=XT_AT + 8192)
        qh = place("qh", [P, TB, 768], at=SPLIT_AT)
        kvh = place("kvh", [P, TB, 1024], at=SPLIT_AT + 6144)
        kcat = place("kcat", [P, TB, 768], at=SPLIT_AT + 14336)
        s_sb = [place(f"s_sb{i}", [P, 384], at=SPLIT_AT + 20480 + 1536 * i) for i in range(2)]
        p_sb = [place(f"p_sb{i}", [P, 384], at=SPLIT_AT + 23552 + 1536 * i) for i in range(2)]
        pT_sb = [place(f"pT_sb{i}", [P, 384], at=SPLIT_AT + 26624 + 1536 * i) for i in range(2)]
        mixT_hi = place("mixT_hi", [P, KM, 256], F32R, at=ARENA)
        mixT_lo = place("mixT_lo", [P, KM, 256], F32R, at=XT_AT)
        fg = place("fg", [P, 4, 256], at=ARENA)
        fT_hi = place("fT_hi", [P, 4, 256], F32R, at=ARENA + 4096)
        fT_lo = place("fT_lo", [P, 4, 256], F32R, at=ARENA + 8192)
        cT = place("cT", [P, 18, 256], at=ARENA)
        kdup = place("kdup", [P, TB, 256], at=ARENA + 18432)
        proj1 = place("proj1", [P, TB, CD_IN], at=ARENA + 24576)
        mix1 = place("mix1", [P, TB, MIX], at=ARENA + 54528)
        sb_buf = [[place(f"sb_{n}{i}", [P, 384], at=SPLIT_AT + 1536 * (4 * j + i)) for i in range(4)]
                  for j, n in enumerate(("abs", "sp", "t", "a"))]
        xe_hi = place("xe_hi", [P, KD, CAP], F32R, at=XT_AT)
        xe_lo = place("xe_lo", [P, KD, CAP], F32R, at=XT_AT + 8192)
        eh = [place(f"eh{i}", [P, FC], at=ARENA + 2048 * i) for i in range(2)]
        hT_hi = place("hT_hi", [P, 4, CAP], F32R, at=ARENA + 4096)
        hT_lo = place("hT_lo", [P, 4, CAP], F32R, at=ARENA + 6144)
        hT32 = place("hT32", [P, 4, CAP], at=ARENA + 4096)
        y_sb = place("y_sb", [P, D], at=ARENA + 8192)
        pick = place("pick", [P, TB, CAP], at=ARENA + 12288)
        pick_g = place("pick_g", [P, TB, CAP], at=ARENA + 13312)
        pick_gT = place("pick_gT", [P, TB, P], at=ARENA + 14336)
        rt = place("rt", [P, 1024], at=ARENA + 15360)
        cnt_i = place("cnt_i", [P, 2], I32, at=ARENA + 19456)
        fgain = place("fgain", [P, D], at=CONST_OFF + 4 * CONST_AT["causal"])
        router_sb = place("router_sb", [P, KD, NE], at=SMALL + 768)

        ss, rms, rstd = small[:, 0:2], small[:, 2:4], small[:, 4:6]
        ss4, rs4, ri4 = small[:, 8:12], small[:, 12:16], small[:, 16:20]
        mx, nm, sm = small[:, 20:52], small[:, 52:84], small[:, 84:116]
        snk, rsm = small[:, 116:148], small[:, 148:180]

        pb = [ctx.enter_context(nc.psum_tensor(f"bank{i}", [P, 512], F32))[:, :] for i in range(8)]

        def sem(name):
            return ctx.enter_context(nc.semaphore(name))

        slot_full = [sem(f"slot_full{s}") for s in range(MOE_SLOTS)]
        hi_ready, split_ready, unit_used, plain_used = (
            sem(n) for n in ("hi_ready", "split_ready", "unit_used", "plain_used"))
        dve_step, act_step = sem("dve_step"), sem("act_step")
        consts_in, x_in, decay_in, router_in, gain_in, out_done = (
            sem(n) for n in ("consts_in", "x_in", "decay_in", "router_in", "gain_in", "out_done"))
        sq_done, rms_done, rstd_done, xn_done, xT_banked, xT_hi_done, xT_done, h_done = (
            sem(n) for n in ("sq_done", "rms_done", "rstd_done", "xn_done", "xT_banked", "xT_hi_done",
                             "xT_done", "h_done"))
        proj_done = sem("proj_done")
        mix_done, mixT_banked, mixT_hi_done, mixT_done, outp_banked = (
            sem(n) for n in ("mix_done", "mixT_banked", "mixT_hi_done", "mixT_done", "outp_banked"))
        lat_rms, lat_scaled, lat_banked, latT_done, qkv_banked, qh_done, kvh_done, nope_done, qrope_done, \
            kcat_done, rqk_done, q_banked, k_banked, r_banked, qT_done, kT_done, rT_done, silu_rg = (
                sem(n) for n in ("lat_rms", "lat_scaled", "lat_banked", "latT_done", "qkv_banked", "qh_done",
                                 "kvh_done", "nope_done", "qrope_done", "kcat_done", "rqk_done", "q_banked",
                                 "k_banked", "r_banked", "qT_done", "kT_done", "rT_done", "silu_rg"))
        s_banked, nm_done, exp_done, pT_banked, pT_done, pv_done = (
            sem(n) for n in ("s_banked", "nm_done", "exp_done", "pT_banked", "pT_done", "pv_done"))
        mla_out = sem("mla_out")
        ret_banked, ret_decayed, ret_out, gn_var, gn_sd = (
            sem(n) for n in ("ret_banked", "ret_decayed", "ret_out", "gn_var", "gn_sd"))
        f_silu, f_prod, f_hi_done, f_lo_done = (
            sem(n) for n in ("f_silu", "f_prod", "f_hi_done", "f_lo_done"))
        kdup_done, cT_banked, cT_act, cT_dve, sink_in, sink_exp, swa_out = (
            sem(n) for n in ("kdup_done", "cT_banked", "cT_act", "cT_dve", "sink_in", "sink_exp", "swa_out"))
        z_banked, abs_done, ln_done, sp_done, acc_banked, t_done, a_done, sb_pv = (
            sem(n) for n in ("z_banked", "abs_done", "ln_done", "sp_done", "acc_banked", "t_done", "a_done",
                             "sb_pv"))
        logits_banked, shifted, exp_logits, sel_done, pos_banked, count_done, moe_done = (
            sem(n) for n in ("logits_banked", "shifted", "exp_logits", "sel_done", "pos_banked", "count_done",
                             "moe_done"))
        prep_done, gather_banked, gather_hi, gathered, pgt_banked, pgt_done, e_silu, e_prod, h_banked, \
            hT_done, hT_lo_done, y_done, sc_banked, sc_done = (
                sem("e_" + n) for n in ("prep", "gather_banked", "gather_hi", "gathered", "pgt_banked",
                                        "pgt_done", "silu", "prod", "h_banked", "hT", "hT_lo", "y",
                                        "sc_banked", "sc_done"))

        posm = rt[:, 0:18].rearrange("p (e t) -> p e t", t=TB)
        gate = rt[:, 18:36].rearrange("p (e t) -> p e t", t=TB)

        class Steps:

            def __init__(self, sem, eng=None):
                self.sem, self.n, self.eng = sem, 0, eng

            def __call__(self, ins):
                self.n += 1
                ins.then_inc(self.sem, 1)

            def settle(self):
                self.eng.wait_ge(self.sem, self.n)

        vs, as_ = Steps(dve_step), Steps(act_step)

        def f32(ap):
            return ap.bitcast(F32)

        def bc(ap, n, at=1):
            shape = list(ap.shape)
            shape.insert(at, n)
            return ap.unsqueeze(at).to_broadcast(shape)

        def mm3(out_, a_hi, a_lo, b_hi, b_lo, first, last, **kw):
            nc.tensor.matmul(out_, a_hi, b_hi, start=first, stop=False, **kw)
            nc.tensor.matmul(out_, a_hi, b_lo, start=False, stop=False, **kw)
            return nc.tensor.matmul(out_, a_lo, b_hi, start=False, stop=last, **kw)

        def hi_unit(act, src, buf, width, full, unit):
            act.wait_ge(*full)
            act.wait_ge(unit_used, unit + 1)
            nc.scalar.activation(w_hi[:, buf, 0:width], src, ACT.Copy).then_inc(hi_ready, 1)

        def lo_unit(dve, src, buf, width, unit):
            dve.wait_ge(hi_ready, unit + 1)
            nc.vector.tensor_tensor(w_lo[:, buf, 0:width], src, f32(w_hi[:, buf, 0:width]),
                                    ALU.subtract).then_inc(split_ready, 1)

        class InProj:

            def __init__(self, layer, w, cols, dst, unit0, loads0):
                self.layer, self.cols, self.dst, self.unit0 = layer, cols, dst, unit0
                self.width = cols // IN_CH
                self.w = w[0].rearrange("(h k p) (i n) -> p h k i n", p=P, k=4, n=2 * self.width)
                self.loads0 = loads0

            def view(self, ap):
                return ap[:, 0:4 * self.width]

            def hi(self, act, i, jj):
                for u in range(4):
                    s = 2 * jj + u // 2
                    src = ring[s][:, (u % 2) * 2 * self.width:(u % 2 + 1) * 2 * self.width]
                    hi_unit(act, src, u, 2 * self.width,
                            (slot_full[s], 16 * (self.loads0 + i + 1)), self.unit0 + 8 * i + 4 * jj + u)

            def evac(self, act, i, jj):
                act.wait_ge(unit_used, self.unit0 + 8 * i + 4 * jj + 4 + NBUF)
                for tb in range(TB):
                    ins = nc.scalar.activation(
                        self.dst[:, tb, bass.ds(i * (2 * self.width) + jj * self.width, self.width)],
                        pb[2 * jj + tb][:, 0:self.width], ACT.Copy)
                ins.then_inc(proj_done, 1)

            def act(self, act):
                self.hi(act, 0, 0)
                with act.Fori(0, IN_CH // 2 - 1) as i:
                    self.hi(act, i, 1)
                    self.evac(act, i, 0)
                    self.hi(act, i + 1, 0)
                    self.evac(act, i, 1)
                n = IN_CH // 2 - 1
                self.hi(act, n, 1)
                self.evac(act, n, 0)
                self.evac(act, n, 1)

            def dve(self, dve):
                with dve.Fori(0, IN_CH // 2) as i:
                    for jj in range(2):
                        for u in range(4):
                            s = 2 * jj + u // 2
                            src = ring[s][:, (u % 2) * 2 * self.width:(u % 2 + 1) * 2 * self.width]
                            lo_unit(dve, src, u, 2 * self.width, self.unit0 + 8 * i + 4 * jj + u)

            def pe(self, pe):
                w = self.width
                with pe.Fori(0, IN_CH // 2) as i:
                    for jj in range(2):
                        pe.wait_ge(proj_done, IN_CH * self.layer + 2 * i + jj + 1)
                        for u in range(4):
                            pe.wait_ge(split_ready, self.unit0 + 8 * i + 4 * jj + u + 1)
                            for kk in range(2):
                                k = 2 * u + kk
                                for tb in range(TB):
                                    t = slice(tb * P, tb * P + P)
                                    ins = mm3(pb[2 * jj + tb][:, 0:w], xT_hi[:, k, t], xT_lo[:, k, t],
                                              w_hi[:, u, kk * w:kk * w + w], w_lo[:, u, kk * w:kk * w + w],
                                              k == 0, k == KD - 1)
                            ins.then_inc(unit_used, 1)

            def load(self, sp, i, jj, half):
                dst = ring[2 * jj + half][:, 0:4 * self.width].rearrange("p (k n) -> p k n", k=4)
                src = self.w[:, half, :, bass.ds(i, 1), jj * self.width:(jj + 1) * self.width].rearrange(
                    "p k a n -> p (k a) n")
                sp.dma_start(dst, src).then_inc(slot_full[2 * jj + half], 16)

            def loads_rest(self, sp):
                with sp.Fori(1, IN_CH // 2) as i:
                    for jj in range(2):
                        for half in range(2):
                            sp.wait_ge(split_ready, self.unit0 + 8 * i - 8 + 4 * jj + 2 * half + 2)
                            self.load(sp, i, jj, half)

        ab = InProj(0, ab_w_in, AB_IN, proj, U_AB_IN, 0)
        cd = InProj(1, cd_w_in, CD_IN, proj1, U_CD_IN, 12)

        def norm_act(act, use, gain, dst):
            if use:
                act.wait_ge(h_done, 4 * use)
            else:
                act.wait_ge(x_in, 16)
                act.wait_ge(consts_in, 16)
            for tb in range(TB):
                nc.scalar.activation(xn[:, tb, :], h[:, tb, :], ACT.Square,
                                     accum_out=ss[:, tb:tb + 1]).then_inc(sq_done, 1)
            act.wait_ge(sq_done, 2 * use + 2)
            nc.scalar.activation(rms, ss, ACT.Sqrt, bias=const("eps"), scale=1.0 / D).then_inc(rms_done, 1)
            for k in range(KD):
                act.wait_ge(xT_banked, 4 * use + k // 2 + 1)
                nc.scalar.activation(dst[:, k, :], pb[k // 2][:, (k % 2) * 256:(k % 2) * 256 + 256], ACT.Copy,
                                     scale=const(gain, k, k + 1)).then_inc(xT_hi_done, 1)

        def norm_dve(dve, use, gain, split=True):
            dve.wait_ge(rms_done, use + 1)
            nc.vector.reciprocal(rstd, rms).then_inc(rstd_done, 1)
            dve.wait_ge(rstd_done, use + 1)
            for tb in range(TB):
                nc.vector.tensor_scalar(xn[:, tb, :], h[:, tb, :], rstd[:, tb:tb + 1], None,
                                        ALU.mult).then_inc(xn_done, 1)
            if split:
                for k in range(KD):
                    dve.wait_ge(xT_hi_done, KD * use + (k // 2) * 2 + 2)
                    nc.vector.scalar_tensor_tensor(
                        out=xT_lo[:, k, :], in0=pb[k // 2][:, (k % 2) * 256:(k % 2) * 256 + 256],
                        scalar=const(gain, k, k + 1), in1=f32(xT_hi[:, k, :]), op0=ALU.mult,
                        op1=ALU.subtract).then_inc(xT_done, 1)

        def norm_pe(pe, use):
            pe.wait_ge(xn_done, 2 * use + 2)
            for b in range(4):
                for kk in range(2):
                    for tb in range(TB):
                        k = 2 * b + kk
                        ins = nc.tensor.transpose(pb[b][:, kk * 256 + tb * P:kk * 256 + tb * P + P],
                                                  xn[:, tb, k * P:k * P + P], const("ident"))
                ins.then_inc(xT_banked, 1)

        def mix_pe(pe, layer, src):
            pe.wait_ge(mix_done, layer + 1)
            for b in range(6):
                for kk in range(2):
                    for tb in range(TB):
                        k = 2 * b + kk
                        ins = nc.tensor.transpose(pb[b][:, kk * 256 + tb * P:kk * 256 + tb * P + P],
                                                  src[:, tb, k * P:k * P + P], const("ident"))
                ins.then_inc(mixT_banked, 1)
            pe.wait_ge(mixT_done, KM * layer + KM)
            unit0 = U_CD_OUT if layer else U_AB_OUT
            for k in range(KM):
                pe.wait_ge(split_ready, unit0 + k + 1)
                for tb in range(TB):
                    for n in range(2):
                        t = slice(tb * P, tb * P + P)
                        w = slice(n * 512, n * 512 + 512)
                        ins = mm3(pb[2 * tb + n], mixT_hi[:, k, t], mixT_lo[:, k, t],
                                  w_hi[:, k % NBUF, w], w_lo[:, k % NBUF, w], k == 0, k == KM - 1)
                ins.then_inc(unit_used, 1)

        OUT_SLOTS = {0: [0, 1, 2, 3, 4, 5], 1: [4, 5, 6, 0, 1, 2]}
        OUT_BEFORE = {0: [4, 4, 4, 4, 1, 1], 1: [9, 9, 1, 16, 16, 16]}

        def mix_act(act, layer, gain):
            for k in range(KM):
                act.wait_ge(mixT_banked, 6 * layer + k // 2 + 1)
                nc.scalar.activation(mixT_hi[:, k, :], pb[k // 2][:, (k % 2) * 256:(k % 2) * 256 + 256], ACT.Copy,
                                     scale=const(gain, k, k + 1)).then_inc(mixT_hi_done, 1)
            unit0 = U_CD_OUT if layer else U_AB_OUT
            for k in range(KM):
                s, before = OUT_SLOTS[layer][k // 2], OUT_BEFORE[layer][k // 2]
                hi_unit(act, ring[s][:, (k % 2) * UNIT:(k % 2 + 1) * UNIT], k % NBUF, UNIT,
                        (slot_full[s], 16 * (before + 1)), unit0 + k)

        def mix_dve(dve, layer, gain):
            for k in range(KM):
                dve.wait_ge(mixT_hi_done, KM * layer + (k // 2) * 2 + 2)
                nc.vector.scalar_tensor_tensor(
                    out=mixT_lo[:, k, :], in0=pb[k // 2][:, (k % 2) * 256:(k % 2) * 256 + 256],
                    scalar=const(gain, k, k + 1), in1=f32(mixT_hi[:, k, :]), op0=ALU.mult,
                    op1=ALU.subtract).then_inc(mixT_done, 1)
            unit0 = U_CD_OUT if layer else U_AB_OUT
            for k in range(KM):
                s = OUT_SLOTS[layer][k // 2]
                lo_unit(dve, ring[s][:, (k % 2) * UNIT:(k % 2 + 1) * UNIT], k % NBUF, UNIT, unit0 + k)
            dve.wait_ge(unit_used, unit0 + KM + NBUF)
            for tb in range(TB):
                for n in range(2):
                    w = slice(n * 512, n * 512 + 512)
                    nc.vector.tensor_tensor(h[:, tb, w], h[:, tb, w], pb[2 * tb + n], ALU.add).then_inc(h_done, 1)

        class Softmax:

            def __init__(self, heads, first, q, k, v, bias, coef, sinks, out_at):
                self.heads, self.first, self.q, self.k, self.v = heads, first, q, k, v
                self.bias, self.coef, self.sinks, self.out_at = bias, coef, sinks, out_at

            def scores(self, pe, i):
                n = self.first + i
                if n >= 2:
                    pe.wait_ge(nm_done, n - 1)
                q, k = self.q(i), self.k(i)
                nc.tensor.matmul(pb[i % 2][:, 0:P], q[:, 0:P], k[:, 0:P], start=True, stop=True)
                nc.tensor.matmul(pb[i % 2][:, P:384], q[:, P:256], k[:, 0:256], start=True,
                                 stop=True).then_inc(s_banked, 1)

            def turn(self, pe, i):
                n = self.first + i
                pe.wait_ge(exp_done, 2 * n + 2)
                if n >= 2:
                    pe.wait_ge(pT_done, n - 1)
                for b in range(3):
                    ins = nc.tensor.transpose(pb[(2, 7)[i % 2]][:, b * P:b * P + P],
                                              p_sb[i % 2][:, b * P:b * P + P], const("ident"))
                ins.then_inc(pT_banked, 1)

            def values(self, pe, i):
                pe.wait_ge(pT_done, self.first + i + 1)
                pT, (o0, o1) = pT_sb[i % 2], self.out_at(i)
                nc.tensor.matmul(o0, pT[:, 0:P], self.v(i, 0), start=True, stop=True)
                nc.tensor.matmul(o1, pT[:, P:2 * P], self.v(i, 0), start=True, stop=False)
                nc.tensor.matmul(o1, pT[:, 2 * P:384], self.v(i, 1), start=False,
                                 stop=True).then_inc(pv_done, 1)

            def pe(self, pe):
                for i in range(self.heads + 2):
                    if i < self.heads:
                        self.scores(pe, i)
                    if 1 <= i <= self.heads:
                        self.turn(pe, i - 1)
                    if i >= 2:
                        self.values(pe, i - 2)

            def dve(self, dve):
                for i in range(self.heads):
                    n = self.first + i
                    dve.wait_ge(s_banked, n + 1)
                    if n >= 2:
                        dve.wait_ge(exp_done, 2 * n - 2)
                    vs(nc.vector.scalar_tensor_tensor(out=s_sb[i % 2], in0=self.bias, scalar=self.coef(i),
                                                      in1=pb[i % 2][:, 0:384], op0=ALU.mult, op1=ALU.add))
                    vs.settle()
                    vs(nc.vector.tensor_reduce(mx[:, 2 * i:2 * i + 1], s_sb[i % 2][:, 0:P], AX, ALU.max))
                    vs(nc.vector.tensor_reduce(mx[:, 2 * i + 1:2 * i + 2], s_sb[i % 2][:, P:384], AX, ALU.max))
                    vs.settle()
                    m = mx[:, 2 * i:2 * i + 2]
                    if self.sinks is None:
                        ins = nc.vector.tensor_scalar(nm[:, 2 * i:2 * i + 2], m, -1.0, None, ALU.mult)
                    else:
                        ins = nc.vector.tensor_scalar(nm[:, 2 * i:2 * i + 2], m, self.sinks[:, i:i + 1], -1.0,
                                                      ALU.max, ALU.mult)
                    ins.then_inc(nm_done, 1)

            def act(self, act):
                for i in range(self.heads + 1):
                    if i < self.heads:
                        n = self.first + i
                        act.wait_ge(nm_done, n + 1)
                        if n >= 2:
                            act.wait_ge(pT_banked, n - 1)
                        for t, (a, b) in enumerate(((0, P), (P, 384))):
                            nc.scalar.activation(p_sb[i % 2][:, a:b], s_sb[i % 2][:, a:b], ACT.Exp,
                                                 bias=nm[:, 2 * i + t:2 * i + t + 1],
                                                 accum_out=sm[:, 2 * i + t:2 * i + t + 1]).then_inc(exp_done, 1)
                    if i >= 1:
                        n = self.first + i - 1
                        act.wait_ge(pT_banked, n + 1)
                        if n >= 2:
                            act.wait_ge(pv_done, n - 1)
                        nc.scalar.activation(pT_sb[(i - 1) % 2], pb[(2, 7)[(i - 1) % 2]][:, 0:384],
                                             ACT.Copy).then_inc(pT_done, 1)

        def half_rows(i):
            return slice((i % 2) * 64, (i % 2) * 64 + 64)

        mla = Softmax(MLA_H, 0, lambda i: qT[0:MLA_D, i, :], lambda i: kT[0:MLA_D, i, :],
                      lambda i, t: kvh[:, t, i * 128 + NOPE:i * 128 + 128], const("causal"), lambda i: 1.0, None,
                      lambda i: (pb[3][:, i * 64:i * 64 + 64], pb[4][:, i * 64:i * 64 + 64]))
        swa = Softmax(SWA_H, MLA_H, lambda i: cT[half_rows(i), i // 2, :],
                      lambda i: cT[half_rows(i), 8 + i // 8, :],
                      lambda i, t: proj1[:, t, C_SV + (i // 8) * 64:C_SV + (i // 8) * 64 + 64], const("dist"),
                      lambda i: -2.0 ** (-8.0 * (i + 1) / SWA_H), const("sinks"),
                      lambda i: (pb[3 + i // 8][:, (i % 8) * 64:(i % 8) * 64 + 64],
                                 pb[5 + i // 8][:, (i % 8) * 64:(i % 8) * 64 + 64]))

        def l0_act(act):
            act.wait_ge(proj_done, IN_CH + 2)
            for tb in range(TB):
                as_(nc.scalar.activation(mix[:, tb, 0:Q_RANK], proj[:, tb, 0:Q_RANK], ACT.Square,
                                         accum_out=ss4[:, tb:tb + 1]))
                as_(nc.scalar.activation(mix[:, tb, Q_RANK:A_KR], proj[:, tb, A_KV:A_KR], ACT.Square,
                                         accum_out=ss4[:, 2 + tb:3 + tb]))
            as_.settle()
            nc.scalar.activation(rs4[:, 0:2], ss4[:, 0:2], ACT.Sqrt, bias=const("eps"),
                                 scale=1.0 / Q_RANK).then_inc(lat_rms, 1)
            nc.scalar.activation(rs4[:, 2:4], ss4[:, 2:4], ACT.Sqrt, bias=const("eps"),
                                 scale=1.0 / KV_RANK).then_inc(lat_rms, 1)
            for tb in range(TB):
                nc.scalar.activation(proj[:, tb, A_RG:AB_IN], proj[:, tb, A_RG:AB_IN],
                                     ACT.Silu).then_inc(silu_rg, 1)
            act.wait_ge(qkv_banked, 1)
            for nh in range(2):
                for tb in range(TB):
                    ins = nc.scalar.activation(qh[:, tb, nh * 384:nh * 384 + 384],
                                               pb[3 + 2 * nh + tb][:, 0:384], ACT.Copy)
            ins.then_inc(qh_done, 1)
            act.wait_ge(qkv_banked, 2)
            for nh in range(2):
                for tb in range(TB):
                    ins = nc.scalar.activation(kvh[:, tb, nh * 512:nh * 512 + 512],
                                               pb[(7, 0, 1, 2)[2 * nh + tb]], ACT.Copy)
            ins.then_inc(kvh_done, 1)
            act.wait_ge(kvh_done, 1)
            for tb in range(TB):
                ins = nc.scalar.activation(
                    kcat[:, tb, :].rearrange("p (h d) -> p h d", d=MLA_D)[:, :, 0:NOPE],
                    kvh[:, tb, :].rearrange("p (h d) -> p h d", d=128)[:, :, 0:NOPE], ACT.Copy)
            ins.then_inc(nope_done, 1)
            act.wait_ge(q_banked, 1)
            for b in range(4):
                ins = nc.scalar.activation(qT[0:MLA_D, 2 * b:2 * b + 2, :].rearrange("p h t -> p (h t)"),
                                           pb[3 + b][0:MLA_D, :], ACT.Copy, scale=MLA_D ** -0.5)
            ins.then_inc(qT_done, 1)
            act.wait_ge(r_banked, 1)
            for b in range(4):
                ins = nc.scalar.activation(rT[:, 2 * b:2 * b + 2, :].rearrange("p h t -> p (h t)"),
                                           pb[3 + b], ACT.Copy)
            ins.then_inc(rT_done, 1)
            mla.act(act)
            act.wait_ge(gn_var, 1)
            nc.scalar.activation(gn_t[:, 128:144],
                                 gn_t[:, 96:128].rearrange("p (g s) -> p g s", s=2)[:, :, 1], ACT.Sqrt,
                                 bias=const("eps")).then_inc(gn_sd, 1)

        def rope(x_, cos, sin, half, a, b, out_, heads=None):
            vs(nc.vector.tensor_tensor(a, x_, cos, ALU.mult))
            vs(nc.vector.tensor_tensor(b[:, :, 0:half], x_[:, :, half:2 * half], sin[:, :, 0:half], ALU.mult))
            vs(nc.vector.tensor_tensor(b[:, :, half:2 * half], x_[:, :, 0:half], sin[:, :, half:2 * half],
                                       ALU.mult))
            vs.settle()
            if heads is not None:
                a, b = (t[:, 0, :].unsqueeze(1).to_broadcast([P, heads, 2 * half]) for t in (a, b))
            return nc.vector.tensor_tensor(out_, a, b, ALU.add)

        def l0_dve(dve):
            dve.wait_ge(lat_rms, 2)
            vs(nc.vector.reciprocal(ri4, rs4))
            vs.settle()
            for tb in range(TB):
                nc.vector.tensor_scalar(proj[:, tb, 0:Q_RANK], proj[:, tb, 0:Q_RANK], ri4[:, tb:tb + 1], None,
                                        ALU.mult).then_inc(lat_scaled, 1)
                nc.vector.tensor_scalar(proj[:, tb, A_KV:A_KR], proj[:, tb, A_KV:A_KR], ri4[:, 2 + tb:3 + tb],
                                        None, ALU.mult).then_inc(lat_scaled, 1)
            dve.wait_ge(unit_used, U_AB_OUT + NBUF)
            t3 = rope_t.rearrange("p (a n) -> p a n", n=32)

            def rot_r(tb):
                ins = rope(proj[:, tb, A_RQK:A_RV].rearrange("p (h d) -> p h d", d=64),
                           bc(const("cos_r", 64 * tb, 64 * tb + 64), 16), bc(const("sin_r", 64 * tb, 64 * tb + 64), 16),
                           32, rqk[:, tb, :].rearrange("p (h d) -> p h d", d=64),
                           rope_t.rearrange("p (h d) -> p h d", d=64),
                           rqk[:, tb, :].rearrange("p (h d) -> p h d", d=64))
                ins.then_inc(rqk_done, 1)
                dve.wait_ge(rqk_done, tb + 1)

            for tb in range(TB):
                ins = rope(proj[:, tb, A_KR:A_RQK].unsqueeze(1), bc(const("cos_m", 32 * tb, 32 * tb + 32), 1),
                           bc(const("sin_m", 32 * tb, 32 * tb + 32), 1), 16, t3[:, 2 * tb:2 * tb + 1, :],
                           t3[:, 2 * tb + 1:2 * tb + 2, :],
                           kcat[:, tb, :].rearrange("p (h d) -> p h d", d=MLA_D)[:, :, NOPE:MLA_D], heads=MLA_H)
                ins.then_inc(kcat_done, 1)
                dve.wait_ge(kcat_done, tb + 1)
            dve.wait_ge(lat_banked, 1)
            for b in range(5):
                ins = nc.vector.tensor_scalar(latT[:, b, :], pb[b // 2][:, (b % 2) * 256:(b % 2) * 256 + 256],
                                              const("g_lat", b, b + 1), None, ALU.mult)
            ins.then_inc(latT_done, 1)
            rot_r(0)
            dve.wait_ge(qh_done, 1)
            for tb in range(TB):
                xq = qh[:, tb, :].rearrange("p (h d) -> p h d", d=MLA_D)[:, :, NOPE:MLA_D]
                ins = rope(xq, bc(const("cos_m", 32 * tb, 32 * tb + 32), 8),
                           bc(const("sin_m", 32 * tb, 32 * tb + 32), 8), 16, t3[:, 0:8, :], t3[:, 8:16, :], xq)
                ins.then_inc(qrope_done, 1)
                dve.wait_ge(qrope_done, tb + 1)
            rot_r(1)
            dve.wait_ge(k_banked, 1)
            for b in range(4):
                ins = nc.vector.tensor_copy(kT[0:MLA_D, 2 * b:2 * b + 2, :].rearrange("p h t -> p (h t)"),
                                            pb[(7, 0, 1, 2)[b]][0:MLA_D, :])
            ins.then_inc(kT_done, 1)
            mla.dve(dve)
            dve.wait_ge(pv_done, MLA_H)
            vs(nc.vector.reciprocal(rsm[:, 0:2 * MLA_H], sm[:, 0:2 * MLA_H]))
            vs.settle()
            r2 = rsm[:, 0:2 * MLA_H].rearrange("p (h t) -> p h t", t=TB)
            for tb in range(TB):
                nc.vector.tensor_tensor(mix[:, tb, 0:512].rearrange("p (h d) -> p h d", d=64),
                                        pb[3 + tb].rearrange("p (h d) -> p h d", d=64),
                                        bc(r2[:, :, tb], 64, 2), ALU.mult).then_inc(mla_out, 1)
            dve.wait_ge(decay_in, 16)
            for i in range(RET_H):
                dve.wait_ge(ret_banked, i + 1)
                if i >= 2:
                    dve.wait_ge(ret_out, i - 1)
                nc.vector.tensor_tensor(s_sb[i % 2][:, 0:256], pb[i % 2][:, 0:256], decay[:, i, :],
                                        ALU.mult).then_inc(ret_decayed, 1)
                nc.vector.tensor_tensor(s_sb[i % 2][:, 256:384], pb[i % 2][:, 256:384], decay[:, i, 0:P],
                                        ALU.mult).then_inc(ret_decayed, 1)
            dve.wait_ge(ret_out, RET_H)
            groups = [(tb, i) for tb in range(TB) for i in range(RET_H)]

            def ret_o(tb, i):
                return pb[3 + 2 * tb + i // 4][:, (i % 4) * P:(i % 4) * P + P]

            for g, (tb, i) in enumerate(groups):
                vs(nc.vector.bn_stats(gn_t[:, 6 * g:6 * g + 6], ret_o(tb, i)))
            vs.settle()
            for g in range(len(groups)):
                ins = nc.vector.bn_aggr(gn_t[:, 96 + 2 * g:98 + 2 * g], gn_t[:, 6 * g:6 * g + 6])
                ins.then_inc(*((gn_var, 1) if g == len(groups) - 1 else (dve_step, 1)))
                vs.n += g != len(groups) - 1
            dve.wait_ge(gn_sd, 1)
            vs(nc.vector.reciprocal(gn_t[:, 144:160], gn_t[:, 128:144]))
            vs.settle()
            for g, (tb, i) in enumerate(groups):
                vs(nc.vector.tensor_scalar(mix[:, tb, 512 + i * P:512 + i * P + P], ret_o(tb, i),
                                           gn_t[:, 96 + 2 * g:97 + 2 * g], gn_t[:, 144 + g:145 + g],
                                           ALU.subtract, ALU.mult))
            vs.settle()
            for tb in range(TB):
                ins = nc.vector.tensor_tensor(mix[:, tb, 512:MIX], mix[:, tb, 512:MIX], proj[:, tb, A_RG:AB_IN],
                                              ALU.mult)
            ins.then_inc(mix_done, 1)

        def l0_pe(pe):
            pe.wait_ge(lat_scaled, 4)
            for b in range(5):
                c0 = b * P
                for tb in range(TB):
                    ins = nc.tensor.transpose(pb[b // 2][:, (b % 2) * 256 + tb * P:(b % 2) * 256 + tb * P + P],
                                              proj[:, tb, c0:c0 + P], const("ident"))
            ins.then_inc(lat_banked, 1)
            pe.wait_ge(latT_done, 1)
            for nh in range(2):
                pe.wait_ge(slot_full[4 + nh], 16)
                for tb in range(TB):
                    for k in range(3):
                        ins = nc.tensor.matmul(pb[3 + 2 * nh + tb][:, 0:384], latT[:, k, tb * P:tb * P + P],
                                               ring[4 + nh][:, k * 384:k * 384 + 384], start=k == 0, stop=k == 2)
            ins.then_inc(qkv_banked, 1)
            pe.wait_ge(slot_full[6], 16)
            for nh in range(2):
                for tb in range(TB):
                    for k in range(2):
                        ins = nc.tensor.matmul(pb[(7, 0, 1, 2)[2 * nh + tb]], latT[:, 3 + k, tb * P:tb * P + P],
                                               ring[6][:, k * 1024 + nh * 512:k * 1024 + nh * 512 + 512],
                                               start=k == 0, stop=k == 1)
            ins.then_inc(qkv_banked, 1)
            pe.wait_ge(qrope_done, 2)
            for i in range(MLA_H):
                for tb in range(TB):
                    c0 = (i % 2) * 256 + tb * P
                    ins = nc.tensor.transpose(pb[3 + i // 2][0:MLA_D, c0:c0 + P],
                                              qh[:, tb, i * MLA_D:i * MLA_D + MLA_D], const("ident"))
            ins.then_inc(q_banked, 1)
            pe.wait_ge(nope_done, 1)
            pe.wait_ge(kcat_done, 2)
            for i in range(MLA_H):
                for tb in range(TB):
                    c0 = (i % 2) * 256 + tb * P
                    ins = nc.tensor.transpose(pb[(7, 0, 1, 2)[i // 2]][0:MLA_D, c0:c0 + P],
                                              kcat[:, tb, i * MLA_D:i * MLA_D + MLA_D], const("ident"))
            ins.then_inc(k_banked, 1)
            pe.wait_ge(qT_done, 1)
            pe.wait_ge(rqk_done, 2)
            for b in range(8):
                for tb in range(TB):
                    c0 = (b % 2) * 256 + tb * P
                    ins = nc.tensor.transpose(pb[3 + b // 2][:, c0:c0 + P], rqk[:, tb, b * P:b * P + P],
                                              const("ident"))
            ins.then_inc(r_banked, 1)
            pe.wait_ge(kT_done, 1)
            pe.wait_ge(rT_done, 1)
            mla.pe(pe)

            def ret_values(i):
                pe.wait_ge(ret_decayed, 2 * i + 2)
                o0, o1 = (pb[3 + 2 * tb + i // 4][:, (i % 4) * P:(i % 4) * P + P] for tb in range(TB))
                v0, v1 = (proj[:, tb, A_RV + i * P:A_RV + i * P + P] for tb in range(TB))
                a = s_sb[i % 2]
                nc.tensor.matmul(o0, a[:, 0:P], v0, start=True, stop=True)
                nc.tensor.matmul(o1, a[:, P:256], v0, start=True, stop=False)
                nc.tensor.matmul(o1, a[:, 256:384], v1, start=False, stop=True).then_inc(ret_out, 1)

            for i in range(RET_H + 1):
                if i < RET_H:
                    if i >= 2:
                        pe.wait_ge(ret_decayed, 2 * i - 2)
                    r = half_rows(i)
                    nc.tensor.matmul(pb[i % 2][:, 0:256], rT[r, 4 + i // 2, 0:P], rT[r, i // 2, :],
                                     start=True, stop=True)
                    nc.tensor.matmul(pb[i % 2][:, 256:384], rT[r, 4 + i // 2, P:256], rT[r, i // 2, P:256],
                                     start=True, stop=True).then_inc(ret_banked, 1)
                if i == 1:
                    pe.wait_ge(mla_out, 2)
                if i >= 1:
                    ret_values(i - 1)

        ZB = (0, 1, 2, 7)

        def l1_act(act):
            for r in range(0, 9, 2):
                act.wait_ge(cT_banked, r + 1)
                nc.scalar.activation(cT[:, 2 * r:2 * r + 2, :].rearrange("p b t -> p (b t)"), pb[r % 8], ACT.Copy,
                                     scale=0.125 if r in (0, 2, 6) else 1.0).then_inc(cT_act, 1)
            swa.act(act)
            act.wait_ge(sink_in, 1)
            nc.scalar.activation(snk, snk, ACT.Exp).then_inc(sink_exp, 1)
            for i in range(SB_H + 2):
                if i < SB_H:
                    b = sb_buf[0][i % 4]
                    act.wait_ge(abs_done, i + 1)
                    as_(nc.scalar.activation(b, b, ACT.Exp))
                    as_.settle()
                    nc.scalar.activation(b, b, ACT.Ln, bias=1.0).then_inc(ln_done, 1)
                if i >= 2:
                    act.wait_ge(t_done, i - 1)
                    if i >= 6:
                        act.wait_ge(sb_pv, i - 5)
                    nc.scalar.activation(sb_buf[3][(i - 2) % 4], sb_buf[2][(i - 2) % 4],
                                         ACT.Exp).then_inc(a_done, 1)

        def l1_dve(dve):
            dve.wait_ge(proj_done, 2 * IN_CH + 2)
            for tb in range(TB):
                nc.vector.tensor_copy(
                    kdup[:, tb, :].rearrange("p (g r d) -> p g r d", g=2, r=2),
                    bc(proj1[:, tb, C_SK:C_SV].rearrange("p (g d) -> p g d", d=HD), 2, 2)).then_inc(kdup_done, 1)
            for r in range(1, 9, 2):
                dve.wait_ge(cT_banked, r + 1)
                o = cT[:, 2 * r:2 * r + 2, :].rearrange("p b t -> p (b t)")
                if r == 7:
                    ins = nc.vector.tensor_copy(o, pb[r])
                else:
                    ins = nc.vector.tensor_scalar(o, pb[r], 0.125, None, ALU.mult)
                ins.then_inc(cT_dve, 1)
            swa.dve(dve)
            n2 = 2 * SWA_H
            dve.wait_ge(nm_done, MLA_H + SWA_H)
            nc.vector.tensor_tensor(snk[:, 0:n2].rearrange("p (h t) -> p h t", t=TB), bc(const("sinks"), TB, 2),
                                    nm[:, 0:n2].rearrange("p (h t) -> p h t", t=TB), ALU.add).then_inc(sink_in, 1)
            dve.wait_ge(sink_exp, 1)
            dve.wait_ge(pv_done, MLA_H + SWA_H)
            vs(nc.vector.tensor_tensor(sm[:, 0:n2], sm[:, 0:n2], snk[:, 0:n2], ALU.add))
            vs.settle()
            vs(nc.vector.reciprocal(rsm[:, 0:n2], sm[:, 0:n2]))
            vs.settle()
            r2 = rsm[:, 0:n2].rearrange("p (h t) -> p h t", t=TB)
            for tb in range(TB):
                for g in range(2):
                    nc.vector.tensor_tensor(mix1[:, tb, 512 * g:512 * g + 512].rearrange("p (h d) -> p h d", d=64),
                                            pb[3 + 2 * tb + g].rearrange("p (h d) -> p h d", d=64),
                                            bc(r2[:, 8 * g:8 * g + 8, tb], 64, 2), ALU.mult).then_inc(swa_out, 1)

            def minus_abs(i):
                dve.wait_ge(z_banked, i + 1)
                z = pb[ZB[i % 4]][:, 0:384]
                if i >= 4:
                    dve.wait_ge(a_done, i - 3)
                    dve.wait_ge(sp_done, i - 3)
                vs(nc.vector.tensor_scalar(sb_buf[2][i % 4], z, -1.0, None, ALU.mult))
                vs.settle()
                nc.vector.tensor_tensor(sb_buf[0][i % 4], sb_buf[2][i % 4], z, ALU.min).then_inc(abs_done, 1)

            def softplus(i):
                dve.wait_ge(ln_done, i + 1)
                if i >= 4:
                    dve.wait_ge(acc_banked, i - 3)
                z, sp_ = pb[ZB[i % 4]][:, 0:384], sb_buf[1][i % 4]
                vs(nc.vector.scalar_tensor_tensor(out=sp_, in0=z, scalar=0.0, in1=sb_buf[0][i % 4], op0=ALU.max,
                                                  op1=ALU.add))
                vs.settle()
                v = sp_.rearrange("p (b q) -> p b q", q=P)[:, 0:3:2, :]
                nc.vector.tensor_tensor(v, v, bc(const("before"), 2), ALU.mult).then_inc(sp_done, 1)

            def masked(i):
                dve.wait_ge(acc_banked, i + 1)
                nc.vector.tensor_tensor(sb_buf[2][i % 4], pb[ZB[i % 4]][:, 0:384], const("sb_neg"),
                                        ALU.add).then_inc(t_done, 1)

            for i in range(SB_H + 2):
                if i < SB_H:
                    minus_abs(i)
                if 1 <= i <= SB_H:
                    softplus(i - 1)
                if i >= 2:
                    masked(i - 2)
            dve.wait_ge(sb_pv, SB_H)
            for tb in range(TB):
                ins = nc.vector.tensor_copy(mix1[:, tb, 1024:MIX], pb[3 + tb])
            ins.then_inc(mix_done, 1)

        def l1_pe(pe):
            pe.wait_ge(proj_done, 2 * IN_CH + 2)
            pe.wait_ge(kdup_done, 2)
            for r in range(9):
                if r == 8:
                    pe.wait_ge(cT_act, 1)
                for kk in range(2):
                    b = 2 * r + kk
                    for tb in range(TB):
                        if b < 8:
                            src = proj1[:, tb, b * P:b * P + P]
                        elif b < 10:
                            src = kdup[:, tb, (b - 8) * P:(b - 8) * P + P]
                        else:
                            src = proj1[:, tb, C_BQ + (b - 10) * P:C_BQ + (b - 10) * P + P]
                        ins = nc.tensor.transpose(pb[r % 8][:, kk * 256 + tb * P:kk * 256 + tb * P + P], src,
                                                  const("ident"))
                ins.then_inc(cT_banked, 1)
            pe.wait_ge(cT_act, 5)
            pe.wait_ge(cT_dve, 4)
            swa.pe(pe)

            def z_scores(i):
                if i >= 4:
                    pe.wait_ge(t_done, i - 3)
                r, z = half_rows(i), pb[ZB[i % 4]]
                q, k = cT[r, 10 + i // 2, :], cT[r, 14 + i // 2, :]
                nc.tensor.matmul(z[:, 0:256], k[:, 0:P], q[:, 0:256], start=True, stop=False,
                                 skip_group_check=True)
                nc.tensor.matmul(z[:, 256:384], k[:, P:256], q[:, P:256], start=False, stop=False,
                                 skip_group_check=True).then_inc(z_banked, 1)

            def log_after(i):
                pe.wait_ge(sp_done, i + 1)
                z, sp_ = pb[ZB[i % 4]], sb_buf[1][i % 4]
                nc.tensor.matmul(z[:, 0:256], const("incl"), sp_[:, 0:256], start=False, stop=False,
                                 skip_group_check=True)
                nc.tensor.matmul(z[:, P:256], const("negones"), sp_[:, 256:384], start=False, stop=False,
                                 skip_group_check=True)
                nc.tensor.matmul(z[:, 256:384], const("incl"), sp_[:, 256:384], start=False, stop=True,
                                 skip_group_check=True).then_inc(acc_banked, 1)

            def weigh(i):
                pe.wait_ge(a_done, i + 1)
                if i == 0:
                    pe.wait_ge(swa_out, 4)
                a = sb_buf[3][i % 4]
                o0, o1 = (pb[3 + tb][:, i * 64:i * 64 + 64] for tb in range(TB))
                v0, v1 = (proj1[:, tb, C_BV + i * 64:C_BV + i * 64 + 64] for tb in range(TB))
                nc.tensor.matmul(o0, a[:, 0:P], v0, start=True, stop=True)
                nc.tensor.matmul(o1, a[:, P:256], v0, start=True, stop=False)
                nc.tensor.matmul(o1, a[:, 256:384], v1, start=False, stop=True).then_inc(sb_pv, 1)

            for i in range(SB_H + 3):
                if i < SB_H:
                    z_scores(i)
                if 1 <= i <= SB_H:
                    log_after(i - 1)
                if i >= 3:
                    weigh(i - 3)

        def f_unit(kind, c):
            if kind == "d":
                return U_FFN + 8 + 12 * c + 4
            return U_FFN + 8 + 12 * (c - 1) + (0 if kind == "g" else 8)

        F_SLOT = dict(g=0, u=2, d=4)
        F_BEFORE = dict(g=5, u=5, d=2)

        def f_src(kind, half, u):
            return ring[F_SLOT[kind] + half][:, u * UNIT:u * UNIT + UNIT]

        def f_load(sp, kind, c, half):
            s = F_SLOT[kind] + half
            if kind == "d":
                dst = ring[s].rearrange("p (k n) -> p k n", k=2)
                src = f_down[0, bass.ds(c * FC + half * 256, 256), :].rearrange("(k p) n -> p k n", p=P)
            else:
                dst = ring[s].rearrange("p (k n) -> p k n", k=4)
                w = f_gate if kind == "g" else f_up
                src = w[0, half * 512:half * 512 + 512, bass.ds(c * FC, FC)].rearrange("(k p) n -> p k n", p=P)
            sp.dma_start(dst, src).then_inc(slot_full[s], 16)

        def f_hi(act, kind, c, first):
            for u in range(4):
                s = F_SLOT[kind] + u // 2
                hi_unit(act, f_src(kind, u // 2, u % 2), u, UNIT, (slot_full[s], 16 * (F_BEFORE[kind] + c + 1)),
                        first + u)

        def f_lo(dve, kind, first):
            for u in range(4):
                lo_unit(dve, f_src(kind, u // 2, u % 2), u, UNIT, first + u)

        def f_gate_up(pe, kind, c, first):
            b0 = 0 if kind == "g" else 2
            for u in range(4):
                pe.wait_ge(split_ready, first + u + 1)
                for kk in range(2):
                    k = 2 * u + kk
                    for j in range(4):
                        w = slice(kk * 512 + j * P, kk * 512 + j * P + P)
                        ins = mm3(pb[b0 + j // 2][:, (j % 2) * 256:(j % 2) * 256 + 256], w_hi[:, u, w],
                                  w_lo[:, u, w], xT_hi[:, k, :], xT_lo[:, k, :], k == 0 and j % 2 == 0,
                                  k == KD - 1, skip_group_check=True)
                ins.then_inc(unit_used, 1)

        def f_down_pe(pe, first, start, stop):
            for t in range(4):
                pe.wait_ge(split_ready, first + t + 1)
                for tb in range(TB):
                    for n in range(2):
                        w, tk = slice(n * 512, n * 512 + 512), slice(tb * P, tb * P + P)
                        ins = mm3(pb[4 + 2 * tb + n], fT_hi[:, t, tk], fT_lo[:, t, tk], w_hi[:, t, w],
                                  w_lo[:, t, w], start and t == 0, stop and t == 3, skip_group_check=True)
                ins.then_inc(unit_used, 1)

        def f_silu_act(act, c, g_end):
            act.wait_ge(unit_used, g_end + NBUF)
            act.wait_ge(f_lo_done, 2 * c + 2)
            for b in range(2):
                nc.scalar.activation(fg[:, 2 * b:2 * b + 2, :].rearrange("p j t -> p (j t)"), pb[b],
                                     ACT.Silu).then_inc(f_silu, 1)

        def f_round(act, c):
            act.wait_ge(f_prod, 2 * c + 2)
            nc.scalar.activation(fT_hi, fg, ACT.Copy).then_inc(f_hi_done, 1)

        def f_prod_dve(dve, c, u_end):
            dve.wait_ge(unit_used, u_end + NBUF)
            for b in range(2):
                dve.wait_ge(f_silu, 2 * c + b + 1)
                v = fg[:, 2 * b:2 * b + 2, :].rearrange("p j t -> p (j t)")
                nc.vector.tensor_tensor(v, v, pb[2 + b], ALU.mult).then_inc(f_prod, 1)

        def f_rest(dve, c):
            dve.wait_ge(f_hi_done, c + 1)
            nc.vector.tensor_tensor(fT_lo, fg, f32(fT_hi), ALU.subtract).then_inc(f_lo_done, 2)

        def ffn_act(act):
            f_hi(act, "g", 0, U_FFN)
            f_hi(act, "u", 0, U_FFN + 4)
            f_silu_act(act, 0, U_FFN + 4)
            with act.Fori(1, NFC) as c:
                f_hi(act, "g", c, f_unit("g", c))
                f_round(act, c - 1)
                f_hi(act, "d", c - 1, f_unit("d", c - 1))
                f_silu_act(act, c, f_unit("g", c) + 4)
                f_hi(act, "u", c, f_unit("u", c))
            f_round(act, NFC - 1)
            f_hi(act, "d", NFC - 1, U_FFN + 8 + 12 * (NFC - 1))

        def ffn_dve(dve):
            f_lo(dve, "g", U_FFN)
            f_lo(dve, "u", U_FFN + 4)
            with dve.Fori(1, NFC) as c:
                f_lo(dve, "g", f_unit("g", c))
                f_prod_dve(dve, c - 1, f_unit("g", c))
                f_rest(dve, c - 1)
                f_lo(dve, "d", f_unit("d", c - 1))
                f_lo(dve, "u", f_unit("u", c))
            f_prod_dve(dve, NFC - 1, U_FFN + 8 + 12 * (NFC - 1))
            f_rest(dve, NFC - 1)
            f_lo(dve, "d", U_FFN + 8 + 12 * (NFC - 1))
            dve.wait_ge(unit_used, U_CD_IN + NBUF)
            for tb in range(TB):
                for n in range(2):
                    w = slice(n * 512, n * 512 + 512)
                    nc.vector.tensor_tensor(h[:, tb, w], h[:, tb, w], pb[4 + 2 * tb + n], ALU.add).then_inc(h_done, 1)

        def ffn_pe(pe):
            pe.wait_ge(xT_done, 2 * KD)
            f_gate_up(pe, "g", 0, U_FFN)
            f_gate_up(pe, "u", 0, U_FFN + 4)

            def middle(c, start):
                pe.wait_ge(f_silu, 2 * c)
                f_gate_up(pe, "g", c, f_unit("g", c))
                pe.wait_ge(f_lo_done, 2 * c + 2)
                f_down_pe(pe, f_unit("d", c - 1), start, False)
                f_gate_up(pe, "u", c, f_unit("u", c))

            middle(1, True)
            with pe.Fori(2, NFC) as c:
                middle(c, False)
            pe.wait_ge(f_lo_done, 2 * NFC + 2)
            f_down_pe(pe, U_FFN + 8 + 12 * (NFC - 1), False, True)

        items = moe_items()
        unit_end, plain_end = {}, {}
        for kind, c, half, how, n in plan:
            (unit_end if how == "split" else plain_end)[kind, c, half] = n
        m_slot = [(m + 7) % MOE_SLOTS for m in range(len(plan))]
        M_BEFORE = [17, 17, 17, 16, 10, 10, 2] + [0] * 7

        def m_loaded(m, q):
            s = m_slot[m]
            return slot_full[s], 16 * (3 * q + (M_BEFORE[s] + m // MOE_SLOTS + 1))

        def m_done(m, q):
            kind, c, half, how, n = plan[m]
            if how == "split":
                return split_ready, UPE * q + (U_MOE + n)
            return plain_used, PPE * q + n

        def m_used(kind, c, q):
            if (kind, c, 1) in unit_end:
                return unit_used, UPE * q + (U_MOE + unit_end[kind, c, 1] + NBUF)
            return plain_used, PPE * q + plain_end[kind, c, 1]

        def m_load(sp, m, e):
            kind, c, half = plan[m][:3]
            s = m_slot[m]
            if kind == "d":
                dst = ring[s].rearrange("p (k n) -> p k n", k=2)
                src = m_down[0, bass.ds(e, 1), c * FC + half * 256:c * FC + half * 256 + 256, :].rearrange(
                    "e (k p) n -> p (e k) n", p=P)
            else:
                dst = ring[s].rearrange("p (k n) -> p k n", k=4)
                w = m_gate if kind == "g" else m_up
                src = w[0, bass.ds(e, 1), half * 512:half * 512 + 512, c * FC:c * FC + FC].rearrange(
                    "e (k p) n -> p (e k) n", p=P)
            sp.dma_start(dst, src).then_inc(slot_full[s], 16)

        def m_loads(sp, lo, hi, e, q):
            for m in range(lo, hi):
                if m < MOE_SLOTS:
                    sp.wait_ge(*m_done(m - MOE_SLOTS + len(plan), q - 1))
                else:
                    sp.wait_ge(*m_done(m - MOE_SLOTS, q))
                m_load(sp, m, e)

        def moe_sp(sp, part):
            n, q0 = len(plan), NE * part
            if part:
                m_loads(sp, 0, MOE_SLOTS, 0, q0)
            with sp.Fori(0, NE - 1) as e:
                m_loads(sp, MOE_SLOTS, n, e, e + q0)
                m_loads(sp, 0, MOE_SLOTS, e + 1, e + (q0 + 1))
            m_loads(sp, MOE_SLOTS, n, NE - 1, q0 + NE - 1)

        def m_src(m, u):
            return ring[m_slot[m]][:, u * UNIT:u * UNIT + UNIT]

        def m_units(item):
            found = []
            for m, (kind, c, half, how, n) in enumerate(plan):
                if (kind, c) == item and how == "split":
                    found += [(m, u, n - 2 + u, (n - 2 + u) % NBUF) for u in range(2)]
            return found

        def m_hi(act, item, q):
            for m, u, n, buf in m_units(item):
                hi_unit(act, m_src(m, u), buf, UNIT, m_loaded(m, q), UPE * q + (U_MOE + n))

        def m_lo(dve, item, q):
            for m, u, n, buf in m_units(item):
                lo_unit(dve, m_src(m, u), buf, UNIT, UPE * q + (U_MOE + n))

        def split_down(c):
            return c in DOWN_SPLIT

        def gather_act(act, r, done):
            act.wait_ge(gather_banked, done)
            for kk in range(4):
                k = 4 * r + kk
                ins = nc.scalar.activation(xe_hi[:, k, :], pb[7][:, kk * P:kk * P + P], ACT.Copy,
                                           scale=const("g_moe", k, k + 1))
            ins.then_inc(gather_hi, 1)

        def gather_dve(dve, r, done):
            dve.wait_ge(gather_hi, done)
            for kk in range(4):
                k = 4 * r + kk
                ins = nc.vector.scalar_tensor_tensor(
                    out=xe_lo[:, k, :], in0=pb[7][:, kk * P:kk * P + P], scalar=const("g_moe", k, k + 1),
                    in1=f32(xe_hi[:, k, :]), op0=ALU.mult, op1=ALU.subtract)
            ins.then_inc(gathered, 1)

        def gather_pe(pe, r):
            for kk in range(4):
                k = 4 * r + kk
                for tb in range(TB):
                    ins = nc.tensor.matmul(pb[7][:, kk * P:kk * P + P], xn[:, tb, k * P:k * P + P],
                                           pick[:, tb, :], start=tb == 0, stop=tb == 1)
            ins.then_inc(gather_banked, 1)

        def prepare(dve, e, part):
            for tb in range(TB):
                place_of = posm[:, bass.ds(e, 1), tb]
                vs_free(nc.vector.tensor_scalar(pick[:, tb, :], const("iota", CAP * part, CAP * part + CAP),
                                                place_of, None, ALU.is_equal))
                vs_free(nc.vector.tensor_scalar(pick_g[:, tb, :], const("iota", CAP * part, CAP * part + CAP),
                                                place_of, gate[:, bass.ds(e, 1), tb], ALU.is_equal, ALU.mult))

        def vs_free(ins):
            ins.then_inc(prep_done, 1)

        def moe_act(act, part):
            q0, g0 = NE * part, 18 * part
            for r in range(2):
                gather_act(act, r, g0 + r + 1)
            with act.Fori(0, NE) as e:
                q = e + q0

                def silu_(c):
                    act.wait_ge(*m_used("g", c, q))
                    act.wait_ge(h_banked, 7 * q + max(c, 1))
                    nc.scalar.activation(eh[c % 2], pb[2 * (c % 2)], ACT.Silu).then_inc(e_silu, 1)

                def turned(c):
                    act.wait_ge(h_banked, 7 * q + (c + 2))
                    dst = hT_hi if split_down(c) else hT32
                    nc.scalar.activation(dst.rearrange("p j t -> p (j t)"), pb[6], ACT.Copy).then_inc(hT_done, 1)

                for kind, c in items:
                    m_hi(act, (kind, c), q)
                    if kind == "g" and c == 1:
                        act.wait_ge(pgt_banked, q + 1)
                        nc.scalar.activation(pick_gT.rearrange("p b t -> p (b t)"), pb[7][:, 0:256],
                                             ACT.Copy).then_inc(pgt_done, 1)
                    if kind == "u":
                        if c:
                            turned(c - 1)
                        silu_(c)
                    if kind == "u" and c == NFC - 1:
                        act.wait_ge(*m_used("u", NFC - 1, q))
                        gather_act(act, 0, 2 * e + (g0 + 3))
                turned(NFC - 1)
                gather_act(act, 1, 2 * e + (g0 + 4))
                act.wait_ge(*m_used("d", NFC - 1, q))
                for n in range(2):
                    ins = nc.scalar.activation(y_sb[:, n * 512:n * 512 + 512], pb[4 + n], ACT.Copy)
                ins.then_inc(y_done, 1)

        def moe_dve(dve, part):
            q0, g0 = NE * part, 18 * part
            prepare(dve, 0, part)
            for r in range(2):
                gather_dve(dve, r, g0 + r + 1)
            with dve.Fori(0, NE) as e:
                q = e + q0

                def product(c):
                    dve.wait_ge(*m_used("u", c, q))
                    dve.wait_ge(e_silu, 7 * q + (c + 1))
                    nc.vector.tensor_tensor(eh[c % 2], eh[c % 2], pb[2 * (c % 2) + 1], ALU.mult).then_inc(e_prod, 1)

                def rest(c):
                    if split_down(c):
                        dve.wait_ge(hT_done, 7 * q + (c + 1))
                        nc.vector.tensor_tensor(hT_lo.rearrange("p j t -> p (j t)"), pb[6],
                                                f32(hT_hi.rearrange("p j t -> p (j t)")),
                                                ALU.subtract).then_inc(hT_lo_done, 1)

                for kind, c in items:
                    m_lo(dve, (kind, c), q)
                    if kind == "g" and c == 1:
                        product(0)
                    if kind == "u" and c:
                        rest(c - 1)
                    if kind == "d" and c < NFC - 2:
                        product(c + 1)
                    if kind == "d" and c == 0:
                        dve.wait_ge(pgt_banked, q + 1)
                        prepare(dve, e + 1, part)
                    if kind == "u" and c == NFC - 1:
                        product(c)
                        gather_dve(dve, 0, 2 * e + (g0 + 3))
                rest(NFC - 1)
                gather_dve(dve, 1, 2 * e + (g0 + 4))
                for s in range(4):
                    tb, w = s // 2, slice((s % 2) * 512, (s % 2) * 512 + 512)
                    dve.wait_ge(sc_banked, 4 * q + (s + 1))
                    nc.vector.tensor_tensor(h[:, tb, w], h[:, tb, w], pb[6 + s % 2], ALU.add).then_inc(sc_done, 1)
            dve.wait_ge(sc_done, 4 * (q0 + NE) + 4)

        def moe_pe(pe, part):
            q0, g0, p0 = NE * part, 18 * part, 4 * (NE + 1) * part
            pe.wait_ge(prep_done, p0 + 4)
            gather_pe(pe, 0)
            pe.wait_ge(gathered, g0 + 1)
            gather_pe(pe, 1)
            with pe.Fori(0, NE) as e:
                q = e + q0

                def hT_ready(c):
                    if split_down(c):
                        return hT_lo_done, len(DOWN_SPLIT) * q + (sorted(DOWN_SPLIT).index(c) + 1)
                    return hT_done, 7 * q + (c + 1)

                def gate_up(kind, c):
                    bank = pb[2 * (c % 2) + (kind == "u")]
                    for m, u, n, buf in m_units((kind, c)):
                        pe.wait_ge(split_ready, UPE * q + (U_MOE + n + 1))
                        for kk in range(2):
                            k = 4 * plan[m][2] + 2 * u + kk
                            w = slice(kk * 512, kk * 512 + 512)
                            ins = mm3(bank, xe_hi[:, k, :], xe_lo[:, k, :], w_hi[:, buf, w], w_lo[:, buf, w],
                                      k == 0, k == KD - 1)
                        ins.then_inc(unit_used, 1)

                def turn(c):
                    pe.wait_ge(e_prod, 7 * q + (c + 2))
                    if c == 0:
                        pe.wait_ge(sc_done, 4 * q + 4)
                    else:
                        pe.wait_ge(*hT_ready(c - 1))
                    for j in range(4):
                        ins = nc.tensor.transpose(pb[6][:, j * P:j * P + P], eh[c % 2][:, j * P:j * P + P],
                                                  const("ident"))
                    ins.then_inc(h_banked, 1)

                def down(c):
                    pe.wait_ge(*hT_ready(c))
                    if c == 0:
                        pe.wait_ge(y_done, q + 1)
                    if split_down(c):
                        for m, u, n, buf in m_units(("d", c)):
                            t = 2 * plan[m][2] + u
                            pe.wait_ge(split_ready, UPE * q + (U_MOE + n + 1))
                            for nn in range(2):
                                w = slice(nn * 512, nn * 512 + 512)
                                ins = mm3(pb[4 + nn], hT_hi[:, t, :], hT_lo[:, t, :], w_hi[:, buf, w],
                                          w_lo[:, buf, w], c == 0 and t == 0, c == NFC - 1 and t == 3)
                            ins.then_inc(unit_used, 1)
                    else:
                        for m, (kind, cc, half, how, n) in enumerate(plan):
                            if (kind, cc) != ("d", c):
                                continue
                            pe.wait_ge(*m_loaded(m, q))
                            for u in range(2):
                                t = 2 * half + u
                                for nn in range(2):
                                    ins = nc.tensor.matmul(
                                        pb[4 + nn], hT32[:, t, :],
                                        ring[m_slot[m]][:, u * UNIT + nn * 512:u * UNIT + nn * 512 + 512],
                                        start=c == 0 and t == 0, stop=c == NFC - 1 and t == 3)
                            ins.then_inc(plain_used, 1)

                for kind, c in items:
                    if kind == "d":
                        if c == NFC - 1:
                            turn(c)
                            pe.wait_ge(gathered, 2 * e + (g0 + 3))
                            gather_pe(pe, 1)
                        down(c)
                        continue
                    if kind == "g" and c == 0:
                        pe.wait_ge(gathered, 2 * e + (g0 + 2))
                    if kind == "g":
                        pe.wait_ge(e_prod, 7 * q + max(c, 1))
                    gate_up(kind, c)
                    if kind == "g" and c:
                        turn(c - 1)
                    if kind == "u" and c == 0:
                        pe.wait_ge(prep_done, 4 * e + (p0 + 4))
                        pe.wait_ge(sc_done, 4 * q + 4)
                        for tb in range(TB):
                            ins = nc.tensor.transpose(pb[7][:, tb * P:tb * P + P], pick_g[:, tb, :],
                                                      const("ident"))
                        ins.then_inc(pgt_banked, 1)
                    if kind == "u" and c == NFC - 1:
                        pe.wait_ge(pgt_done, q + 1)
                        pe.wait_ge(prep_done, 4 * e + (p0 + 8))
                        gather_pe(pe, 0)
                pe.wait_ge(y_done, q + 2)
                for s in range(4):
                    if s == 1:
                        pe.wait_ge(gathered, 2 * e + (g0 + 4))
                    if s >= 2:
                        pe.wait_ge(sc_done, 4 * q + (4 + s - 1))
                    nc.tensor.matmul(pb[6 + s % 2], pick_gT[:, s // 2, :],
                                     y_sb[:, (s % 2) * 512:(s % 2) * 512 + 512], start=True,
                                     stop=True).then_inc(sc_banked, 1)

        lg, gt, eq, rank, sel = (rt[:, a:b] for a, b in ((36, 52), (64, 192), (192, 320), (320, 336), (336, 352)))
        lmax, shf, ex, num, den, rden, cmax, pos1 = (
            rt[:, a:b] for a, b in ((352, 354), (356, 372), (372, 388), (388, 404), (404, 406), (406, 408),
                                    (408, 409), (412, 428)))

        def route_pe(pe):
            pe.wait_ge(router_in, 16)
            pe.wait_ge(xT_hi_done, 4 * KD)
            for tb in range(TB):
                for k in range(KD):
                    ins = nc.tensor.matmul(pb[4][:, tb * NE:tb * NE + NE], xT32[:, k, tb * P:tb * P + P],
                                           router_sb[:, k, :], start=k == 0, stop=k == KD - 1)
            ins.then_inc(logits_banked, 1)
            pe.wait_ge(sel_done, 1)
            s0, s1 = sel[:, 0:NE], sel[:, NE:2 * NE]
            nc.tensor.matmul(pb[5][:, 0:8], const("strict"), s0, start=True, stop=True)
            nc.tensor.matmul(pb[5][:, 8:16], const("ones"), s0, start=True, stop=False)
            nc.tensor.matmul(pb[5][:, 8:16], const("strict"), s1, start=False, stop=True)
            nc.tensor.matmul(pb[5][:, 16:24], const("ones"), s0, start=True, stop=False)
            nc.tensor.matmul(pb[5][:, 16:24], const("ones"), s1, start=False, stop=True).then_inc(pos_banked, 1)

        def route_act(act):
            act.wait_ge(shifted, 2)
            nc.scalar.activation(ex, shf, ACT.Exp).then_inc(exp_logits, 1)

        def route_dve(dve):
            dve.wait_ge(logits_banked, 1)
            vs(nc.vector.tensor_copy(lg, pb[4][:, 0:16]))
            vs.settle()
            for tb in range(TB):
                l = lg[:, tb * NE:tb * NE + NE]
                g3 = gt[:, 64 * tb:64 * tb + 64].rearrange("p (j i) -> p j i", i=NE)
                e3 = eq[:, 64 * tb:64 * tb + 64].rearrange("p (j i) -> p j i", i=NE)
                vs(nc.vector.tensor_tensor(g3, bc(l, NE, 1), bc(l, NE, 2), ALU.is_gt))
                vs(nc.vector.tensor_tensor(e3, bc(l, NE, 1), bc(l, NE, 2), ALU.is_equal))
            vs(nc.vector.tensor_reduce(lmax, lg.rearrange("p (t e) -> p t e", e=NE), AX, ALU.max))
            vs.settle()
            for tb in range(TB):
                e2 = eq[:, 64 * tb:64 * tb + 64]
                vs(nc.vector.tensor_tensor(e2, e2, const("lower8"), ALU.mult))
                nc.vector.tensor_scalar(shf[:, tb * NE:tb * NE + NE], lg[:, tb * NE:tb * NE + NE],
                                        lmax[:, tb:tb + 1], None, ALU.subtract).then_inc(shifted, 1)
            vs.settle()
            vs(nc.vector.tensor_tensor(gt, gt, eq, ALU.add))
            vs.settle()
            vs(nc.vector.tensor_reduce(rank, gt.rearrange("p (j i) -> p j i", i=NE), AX, ALU.add))
            vs.settle()
            nc.vector.tensor_scalar(sel, rank, 2.0, None, ALU.is_lt).then_inc(sel_done, 1)
            dve.wait_ge(sel_done, 1)
            dve.wait_ge(exp_logits, 1)
            vs(nc.vector.tensor_tensor(num, ex, sel, ALU.mult))
            vs(nc.vector.memset(posm[:, NE, :], -1.0))
            vs(nc.vector.memset(gate[:, NE, :], 0.0))
            vs.settle()
            vs(nc.vector.tensor_reduce(den, num.rearrange("p (t e) -> p t e", e=NE), AX, ALU.add))
            vs.settle()
            vs(nc.vector.reciprocal(rden, den))
            dve.wait_ge(pos_banked, 1)
            vs(nc.vector.tensor_reduce(cmax, pb[5][:, 16:24], AX, ALU.max))
            vs(nc.vector.scalar_tensor_tensor(out=pos1, in0=pb[5][:, 0:16], scalar=1.0, in1=sel, op0=ALU.add,
                                              op1=ALU.mult))
            vs.settle()
            for tb in range(TB):
                vs(nc.vector.tensor_scalar(gate[:, 0:NE, tb], num[:, tb * NE:tb * NE + NE], rden[:, tb:tb + 1],
                                           None, ALU.mult))
                vs(nc.vector.tensor_scalar(posm[:, 0:NE, tb], pos1[:, tb * NE:tb * NE + NE], -1.0, None, ALU.add))
            vs.settle()
            nc.vector.tensor_copy(cnt_i[:, 0:1], cmax).then_inc(count_done, 1)

        def overflow(eng, body):
            eng.wait_ge(count_done, 1)
            most = eng.value_load(cnt_i[0:1, 0:1], min_val=0, max_val=256)
            with eng.If(most > CAP):
                body(eng, 1)

        block = ctx.enter_context(nc.Block())

        @block.sync
        def _(sp):
            sp.dma_start(h, x[0].rearrange("(b p) d -> p b d", p=P)).then_inc(x_in, 16)
            sp.dma_start(cst, consts).then_inc(consts_in, 16)
            for jj in range(2):
                for half in range(2):
                    ab.load(sp, 0, jj, half)
            for nh in range(2):
                sp.dma_start(ring[4 + nh][:, 0:1152].rearrange("p (k n) -> p k n", k=3),
                             w_uq[0].rearrange("(k p) n -> p k n", p=P)[:, :, nh * 384:nh * 384 + 384]).then_inc(
                                 slot_full[4 + nh], 16)
            sp.dma_start(ring[6].rearrange("p (k n) -> p k n", k=2),
                         w_ukv[0].rearrange("(k p) n -> p k n", p=P)).then_inc(slot_full[6], 16)
            sp.dma_start(router_sb, router[0].rearrange("(k p) e -> p k e", p=P)).then_inc(router_in, 16)
            ab.loads_rest(sp)

            def out_load(w, layer, i):
                s = OUT_SLOTS[layer][i]
                sp.dma_start(ring[s].rearrange("p (k n) -> p k n", k=2),
                             w[0, 256 * i:256 * i + 256, :].rearrange("(k p) n -> p k n", p=P)).then_inc(
                                 slot_full[s], 16)

            for i in range(4):
                sp.wait_ge(split_ready, U_AB_IN + 24 + 2 * i + 2)
                out_load(ab_w_out, 0, i)
            sp.wait_ge(unit_used, U_AB_OUT + NBUF)
            sp.dma_start(decay, decay_t).then_inc(decay_in, 16)
            sp.wait_ge(qkv_banked, 1)
            for i in range(4, 6):
                out_load(ab_w_out, 0, i)
            for kind, i0 in (("g", 0), ("u", 2)):
                for half in range(2):
                    sp.wait_ge(split_ready, U_AB_OUT + 2 * (i0 + half) + 2)
                    f_load(sp, kind, 0, half)
            for kind in "gdu":
                for half in range(2):
                    done = {"g": U_FFN, "d": U_AB_OUT + 8, "u": U_FFN + 4}[kind] + 2 * half + 2
                    sp.wait_ge(split_ready, done)
                    f_load(sp, kind, 0 if kind == "d" else 1, half)
            with sp.Fori(2, NFC) as c:
                for kind in "gdu":
                    cc = c - 1 if kind == "d" else c
                    for half in range(2):
                        sp.wait_ge(split_ready, f_unit(kind, cc - 1) + (2 * half + 2))
                        f_load(sp, kind, cc, half)
            for half in range(2):
                sp.wait_ge(split_ready, f_unit("d", NFC - 2) + 2 * half + 2)
                f_load(sp, "d", NFC - 1, half)
            for jj, kind in enumerate("gu"):
                for half in range(2):
                    sp.wait_ge(split_ready, f_unit(kind, NFC - 1) + 2 * half + 2)
                    cd.load(sp, 0, jj, half)
            cd.loads_rest(sp)
            d6 = U_FFN + 8 + 12 * (NFC - 1)
            for i, done in enumerate((d6 + 2, d6 + 4, None, U_CD_IN + 26, U_CD_IN + 28, U_CD_IN + 30)):
                if done is None:
                    sp.wait_ge(qkv_banked, 2)
                else:
                    sp.wait_ge(split_ready, done)
                out_load(cd_w_out, 1, i)
            sp.wait_ge(mixT_done, 2 * KM)
            sp.dma_start(fgain, final_gain).then_inc(gain_in, 16)
            for m in range(MOE_SLOTS):
                s = m_slot[m]
                if s < 7:
                    last = {4: 2, 5: 4, 6: 6, 0: 8, 1: 10, 2: 12}.get(s, 0)
                    sp.wait_ge(split_ready, U_CD_OUT + last)
                m_load(sp, m, 0)
            moe_sp(sp, 0)
            overflow(sp, moe_sp)
            sp.wait_ge(xn_done, 10)
            sp.dma_start(out[0].rearrange("(b p) d -> p b d", p=P), xn).then_inc(out_done, 16)
            sp.wait_ge(out_done, 16)

        @block.scalar
        def _(act):
            as_.eng = act
            norm_act(act, 0, "g_ab", xT_hi)
            ab.act(act)
            l0_act(act)
            mix_act(act, 0, "g_mix")
            norm_act(act, 1, "g_ffn", xT_hi)
            ffn_act(act)
            norm_act(act, 2, "g_cd", xT_hi)
            cd.act(act)
            l1_act(act)
            mix_act(act, 1, "g_one")
            norm_act(act, 3, "g_moe", xT32)
            route_act(act)
            moe_act(act, 0)
            overflow(act, moe_act)
            act.wait_ge(moe_done, 1)
            for tb in range(TB):
                nc.scalar.activation(xn[:, tb, :], h[:, tb, :], ACT.Square,
                                     accum_out=ss[:, tb:tb + 1]).then_inc(sq_done, 1)
            act.wait_ge(sq_done, 10)
            nc.scalar.activation(rms, ss, ACT.Sqrt, bias=const("eps"), scale=1.0 / D).then_inc(rms_done, 1)

        @block.tensor
        def _(pe):
            pe.sem_inc(unit_used, NBUF)
            pe.sem_inc(h_banked, 1)
            norm_pe(pe, 0)
            pe.wait_ge(xT_done, KD)
            ab.pe(pe)
            l0_pe(pe)
            mix_pe(pe, 0, mix)
            norm_pe(pe, 1)
            ffn_pe(pe)
            norm_pe(pe, 2)
            pe.wait_ge(xT_done, 3 * KD)
            cd.pe(pe)
            l1_pe(pe)
            mix_pe(pe, 1, mix1)
            norm_pe(pe, 3)
            route_pe(pe)
            moe_pe(pe, 0)
            overflow(pe, moe_pe)

        @block.vector
        def _(dve):
            vs.eng = dve
            dve.sem_inc(f_lo_done, 2)
            dve.sem_inc(e_prod, 1)
            dve.sem_inc(sc_done, 4)
            dve.sem_inc(y_done, 1)
            dve.sem_inc(proj_done, 2)
            dve.wait_ge(x_in, 16)
            dve.wait_ge(consts_in, 16)
            norm_dve(dve, 0, "g_ab")
            ab.dve(dve)
            l0_dve(dve)
            mix_dve(dve, 0, "g_mix")
            norm_dve(dve, 1, "g_ffn")
            ffn_dve(dve)
            norm_dve(dve, 2, "g_cd")
            cd.dve(dve)
            l1_dve(dve)
            mix_dve(dve, 1, "g_one")
            norm_dve(dve, 3, "g_moe", split=False)
            route_dve(dve)
            moe_dve(dve, 0)
            overflow(dve, moe_dve)
            dve.wait_ge(gain_in, 16)
            dve.sem_inc(moe_done, 1)
            dve.wait_ge(rms_done, 5)
            nc.vector.reciprocal(rstd, rms).then_inc(rstd_done, 1)
            dve.wait_ge(rstd_done, 5)
            for tb in range(TB):
                nc.vector.scalar_tensor_tensor(out=xn[:, tb, :], in0=h[:, tb, :], scalar=rstd[:, tb:tb + 1],
                                               in1=fgain, op0=ALU.mult, op1=ALU.mult).then_inc(xn_done, 1)


def shape_tables(np):
    i = np.arange(P)
    row, col = i[:, None], i[None, :]
    f = np.float32
    t = {}
    t["ident"] = (row == col).astype(f)
    t["incl"] = -(row >= col).astype(f)
    t["negones"] = -np.ones((P, P), f)
    t["ones"] = np.ones((P, P), f)
    t["before"] = (row < col).astype(f)
    t["strict"] = (row < col).astype(f)
    t["iota"] = np.broadcast_to(np.arange(256, dtype=f), (P, 256))

    def rotary(half):
        inv = (10000.0 ** (-np.arange(half, dtype=f) / half)).astype(f)
        ang = (np.arange(256, dtype=f)[:, None] * inv[None, :]).astype(np.float64)
        c, s = np.cos(ang).astype(f), np.sin(ang).astype(f)
        c, s = np.concatenate([c, c], 1), np.concatenate([-s, s], 1)
        return [m.reshape(2, P, 2 * half).transpose(1, 0, 2).reshape(P, 4 * half) for m in (c, s)]

    t["cos_m"], t["sin_m"] = rotary(16)
    t["cos_r"], t["sin_r"] = rotary(32)
    diag = np.where(col > row, f(MASKED), f(0))
    zero = np.zeros((P, P), f)
    t["causal"] = np.concatenate([diag, zero, diag], 1)
    d0 = np.where(col > row, f(-MASKED), (row - col).astype(f))
    d1 = np.where(col > row, (row + P - col).astype(f), f(-MASKED))
    t["dist"] = np.concatenate([d0, d1, d0], 1)
    neg = np.where(row >= col, f(MASKED), f(0))
    t["sb_neg"] = np.concatenate([neg, zero, neg], 1)
    e = np.arange(8)
    t["lower8"] = np.broadcast_to((e[None, :] < e[:, None]).astype(f).reshape(1, 64), (P, 64))
    t["g_one"] = np.ones((P, KM), f)
    t["eps"] = np.full((P, 1), EPS, f)
    lg = np.log1p(-(2.0 ** (-5.0 - np.arange(RET_H))))
    rel = np.arange(256)[None, None, :] - i[:, None, None]
    decay = np.where(rel >= 0, np.exp(lg[None, :, None] * np.maximum(rel, 0)), 0.0) * RET_DK ** -0.5
    return t, decay.astype(f)


def kernel(**inputs):
    import numpy as np
    import concourse.bacc as bacc
    from concourse.bass_utils import run_bass_kernel_spmd as run

    a = {k: np.asarray(v) for k, v in inputs.items()}
    t, decay = shape_tables(np)

    def columns(g):
        return g.reshape(-1, P).T

    t["g_ab"], t["g_ffn"] = columns(a["ab_norm"][0]), columns(a["ffn_norm"][0])
    t["g_cd"], t["g_moe"] = columns(a["cd_norm"][0]), columns(a["moe_norm"][0])
    t["g_lat"] = np.concatenate([columns(a["mla_q_norm"][0]), columns(a["mla_kv_norm"][0])], 1)
    t["g_mix"] = np.concatenate([np.ones((P, 4), np.float32), columns(a["ret_gn"][0])], 1)
    t["sinks"] = np.broadcast_to(a["swa_sinks"][0][None, :], (P, SWA_H))
    consts = np.ascontiguousarray(np.concatenate([t[n] for n in CONST_WIDTHS], 1))
    assert consts.shape == (P, NCONST) and consts.dtype == np.float32

    nc = bacc.Bacc("TRN2", target_bir_lowering=False, num_devices=1)
    given = dict(x=a["x"], consts=consts, decay=decay, ab_w_in=a["ab_w_in"], w_uq=a["mla_w_uq"],
                 w_ukv=a["mla_w_ukv"], ab_w_out=a["ab_w_out"], f_gate=a["ffn_w_gate"], f_up=a["ffn_w_up"],
                 f_down=a["ffn_w_down"], cd_w_in=a["cd_w_in"], cd_w_out=a["cd_w_out"], router=a["moe_router"],
                 m_gate=a["moe_w_gate"], m_up=a["moe_w_up"], m_down=a["moe_w_down"],
                 final_gain=np.broadcast_to(a["final_norm"][None, :], (P, D)))
    arrays, aps = {}, []
    for name, v in given.items():
        arrays[name + "_dram"] = v = np.ascontiguousarray(v)
        aps.append(nc.dram_tensor(name + "_dram", v.shape, mybir.dt.from_np(v.dtype), kind="ExternalInput").ap())
    out = nc.dram_tensor("out_dram", (1, 256, D), F32, kind="ExternalOutput").ap()
    trunk(nc, *aps, out)
    r = run(nc, [arrays], core_ids=[0])
    return r.results[0]["out_dram"]
```

```python
from contextlib import ExitStack

import concourse.bass as bass
from concourse import mybir

F32 = mybir.dt.float32
F32R = mybir.dt.float32r
I32 = mybir.dt.int32
ALU = mybir.AluOpType
ACT = mybir.ActivationFunctionType
AX = mybir.AxisListType.X

P = 128
TB = 2
D = 1024
KD = D // P
EPS = 1e-6
MASKED = -1e30

Q_RANK, KV_RANK, ROPE = 384, 256, 32
RET_H, RET_DK, RET_DV = 8, 64, 128
AB_IN = 3744
A_KV, A_KR, A_RQK, A_RV, A_RG = 384, 640, 672, 1696, 2720
MLA_H, MLA_D, NOPE = 8, 96, 64
CD_IN = 2816
SWA_H, SWA_KV, HD = 16, 2, 64
C_SK, C_SV, C_BQ, C_BK, C_BV = 1024, 1152, 1280, 1792, 2304
SB_H = 8
MIX = 1536
KM = MIX // P
FF = 3584
FC = 512
NFC = FF // FC
NE = 8
CAP = 128

IN_CH = 8
UNIT = 1024
NBUF = 4
SLOT = 2048
SLOT_BYTES = SLOT * 4

U_AB_IN = 0
U_AB_OUT = U_AB_IN + 4 * IN_CH
U_FFN = U_AB_OUT + KM
U_CD_IN = U_FFN + 12 * NFC
U_CD_OUT = U_CD_IN + 4 * IN_CH
U_MOE = U_CD_OUT + KM
MOE_SLOTS = 14


def moe_items():
    items = [("g", 0), ("u", 0)]
    for c in range(1, NFC):
        items += [("g", c), ("u", c), ("d", c - 1)]
    return items + [("d", NFC - 1)]


CONST_WIDTHS = dict(
    ident=128, incl=128, negones=128, ones=128, before=128, strict=128, iota=256, cos_m=64, sin_m=64,
    cos_r=128, sin_r=128, causal=384, dist=384, sb_neg=384, lower8=64, g_ab=8, g_lat=5, g_mix=12,
    g_ffn=8, g_cd=8, g_one=12, g_moe=8, sinks=16, eps=1)
CONST_AT, _at = {}, 0
for _name, _w in CONST_WIDTHS.items():
    CONST_AT[_name] = _at
    _at += _w
NCONST = _at


def trunk(nc, x, consts, decay_t, ab_w_in, w_uq, w_ukv, ab_w_out, f_gate, f_up, f_down,
          cd_w_in, cd_w_out, router, m_gate, m_up, m_down, moe_gain, final_gain, out):
    with ExitStack() as ctx:
        base = 16640

        def place(name, shape, dt=F32, at=None):
            return nc.alloc_sbuf_tensor_at(name, shape, dt, offset=base + at)[tuple(slice(None) for _ in shape)]

        H_AT, XN_AT, XT_AT, SPLIT_AT = 0, 8192, 16384, 32768
        RING_AT = SPLIT_AT + 32768
        CONST_BYTES = 4 * NCONST
        CONST_OFF = RING_AT + 7 * SLOT_BYTES
        ARENA = CONST_OFF + (CONST_BYTES + 63) // 64 * 64 + 1024
        SMALL = ARENA - 1024
        RINGB_AT = (229344 - base - 7 * SLOT_BYTES) // 64 * 64
        assert RINGB_AT >= ARENA + 19968, (RINGB_AT, ARENA)

        h = place("h", [P, TB, D], at=H_AT)
        xn = place("xn", [P, TB, D], at=XN_AT)
        xT_hi = place("xT_hi", [P, KD, 256], F32R, at=XT_AT)
        xT_lo = place("xT_lo", [P, KD, 256], F32R, at=XT_AT + 8192)
        xT32 = place("xT32", [P, KD, 256], at=XT_AT)
        w_hi = place("w_hi", [P, NBUF, UNIT], F32R, at=SPLIT_AT)
        w_lo = place("w_lo", [P, NBUF, UNIT], F32R, at=SPLIT_AT + 16384)
        ring = [place(f"ring{s}", [P, SLOT], at=RING_AT + s * SLOT_BYTES) for s in range(7)]
        ring += [place(f"ring{s + 7}", [P, SLOT], at=RINGB_AT + s * SLOT_BYTES) for s in range(7)]
        cst = place("cst", [P, NCONST], at=CONST_OFF)
        small = place("small", [P, 256], at=SMALL)

        def const(name, a=0, b=None):
            o = CONST_AT[name]
            return cst[:, o + a:o + (CONST_WIDTHS[name] if b is None else b)]

        qT = place("qT", [P, MLA_H, 256], at=ARENA)
        kT = place("kT", [P, MLA_H, 256], at=ARENA + 8192)
        rT = place("rT", [P, 8, 256], at=ARENA + 16384)
        proj = place("proj", [P, TB, AB_IN], at=ARENA + 24576)
        mix = place("mix", [P, TB, MIX], at=ARENA + 54528)
        latT = place("latT", [P, 5, 256], at=ARENA + 66816)
        rope_t = place("rope_t", [P, 1024], at=ARENA + 71936)
        gn_t = place("gn_t", [P, 256], at=ARENA + 76032)
        assert ARENA + 77056 <= 229344 - base
        decay = place("decay", [P, RET_H, 256], at=XT_AT)
        rqk = place("rqk", [P, TB, 1024], at=XT_AT + 8192)
        qh = place("qh", [P, TB, 768], at=SPLIT_AT)
        kvh = place("kvh", [P, TB, 1024], at=SPLIT_AT + 6144)
        kcat = place("kcat", [P, TB, 768], at=SPLIT_AT + 14336)
        s_sb = [place(f"s_sb{i}", [P, 384], at=SPLIT_AT + 20480 + 1536 * i) for i in range(2)]
        p_sb = [place(f"p_sb{i}", [P, 384], at=SPLIT_AT + 23552 + 1536 * i) for i in range(2)]
        pT_sb = [place(f"pT_sb{i}", [P, 384], at=SPLIT_AT + 26624 + 1536 * i) for i in range(2)]
        mixT_hi = place("mixT_hi", [P, KM, 256], F32R, at=ARENA)
        mixT_lo = place("mixT_lo", [P, KM, 256], F32R, at=XT_AT)
        fg = place("fg", [P, 4, 256], at=ARENA)
        fT_hi = place("fT_hi", [P, 4, 256], F32R, at=ARENA + 4096)
        fT_lo = place("fT_lo", [P, 4, 256], F32R, at=ARENA + 8192)
        cT = place("cT", [P, 18, 256], at=ARENA)
        kdup = place("kdup", [P, TB, 256], at=ARENA + 18432)
        proj1 = place("proj1", [P, TB, CD_IN], at=ARENA + 24576)
        mix1 = place("mix1", [P, TB, MIX], at=ARENA + 54528)
        sb_buf = [[place(f"sb_{n}{i}", [P, 384], at=SPLIT_AT + 1536 * (3 * j + i)) for i in range(3)]
                  for j, n in enumerate(("abs", "sp", "t", "a"))]
        xe_hi = place("xe_hi", [P, KD, CAP], F32R, at=XT_AT)
        xe_lo = place("xe_lo", [P, KD, CAP], F32R, at=XT_AT + 8192)
        eh = [place(f"eh{i}", [P, FC], at=ARENA + 2048 * i) for i in range(2)]
        hT_hi = place("hT_hi", [P, 4, CAP], F32R, at=ARENA + 4096)
        hT_lo = place("hT_lo", [P, 4, CAP], F32R, at=ARENA + 6144)
        g_moe_row = place("g_moe_row", [P, D], at=XT_AT + 12288)
        y_sb = place("y_sb", [P, D], at=ARENA + 8192)
        pick = place("pick", [P, TB, CAP], at=ARENA + 12288)
        pick_g = place("pick_g", [P, TB, CAP], at=ARENA + 13312)
        pick_gT = place("pick_gT", [P, TB, P], at=ARENA + 14336)
        rt = place("rt", [P, 1024], at=ARENA + 15360)
        cnt_i = place("cnt_i", [P, 2], I32, at=ARENA + 19456)
        fgain = place("fgain", [P, D], at=CONST_OFF + 4 * CONST_AT["causal"])
        router_sb = place("router_sb", [P, KD, NE], at=SMALL + 768)

        ss, rms, rstd = small[:, 0:2], small[:, 2:4], small[:, 4:6]
        ss4, rs4, ri4 = small[:, 8:12], small[:, 12:16], small[:, 16:20]
        mx, nm, sm = small[:, 20:52], small[:, 52:84], small[:, 84:116]
        snk, rsm = small[:, 116:148], small[:, 148:180]

        pb = [ctx.enter_context(nc.psum_tensor(f"bank{i}", [P, 512], F32))[:, :] for i in range(8)]

        def sem(name):
            return ctx.enter_context(nc.semaphore(name))

        slot_full = [sem(f"slot_full{s}") for s in range(MOE_SLOTS)]
        hi_ready, split_ready, unit_used = (sem(n) for n in ("hi_ready", "split_ready", "unit_used"))
        dve_step, act_step = sem("dve_step"), sem("act_step")
        consts_in, x_in, decay_in, router_in, gain_in, g_moe_in, rows_scaled, out_done = (
            sem(n) for n in ("consts_in", "x_in", "decay_in", "router_in", "gain_in", "g_moe_in", "rows_scaled",
                             "out_done"))
        sq_done, rms_done, rstd_done, xn_done, xT_banked, xT_hi_done, xT_done, h_done = (
            sem(n) for n in ("sq_done", "rms_done", "rstd_done", "xn_done", "xT_banked", "xT_hi_done",
                             "xT_done", "h_done"))
        proj_done = sem("proj_done")
        mix_done, mixT_banked, mixT_hi_done, mixT_done, outp_banked = (
            sem(n) for n in ("mix_done", "mixT_banked", "mixT_hi_done", "mixT_done", "outp_banked"))
        lat_rms, lat_scaled, lat_banked, latT_done, qkv_banked, qh_done, kvh_done, nope_done, qrope_done, \
            kcat_done, rqk_done, q_banked, k_banked, r_banked, qT_done, kT_done, rT_done, silu_rg = (
                sem(n) for n in ("lat_rms", "lat_scaled", "lat_banked", "latT_done", "qkv_banked", "qh_done",
                                 "kvh_done", "nope_done", "qrope_done", "kcat_done", "rqk_done", "q_banked",
                                 "k_banked", "r_banked", "qT_done", "kT_done", "rT_done", "silu_rg"))
        s_banked, nm_done, exp_done, pT_banked, pT_done, pv_done = (
            sem(n) for n in ("s_banked", "nm_done", "exp_done", "pT_banked", "pT_done", "pv_done"))
        mla_out = sem("mla_out")
        ret_banked, ret_decayed, ret_out, gn_var, gn_sd = (
            sem(n) for n in ("ret_banked", "ret_decayed", "ret_out", "gn_var", "gn_sd"))
        f_silu, f_prod, f_hi_done, f_lo_done = (
            sem(n) for n in ("f_silu", "f_prod", "f_hi_done", "f_lo_done"))
        kdup_done, cT_banked, cT_act, cT_dve, sink_in, sink_exp, swa_out = (
            sem(n) for n in ("kdup_done", "cT_banked", "cT_act", "cT_dve", "sink_in", "sink_exp", "swa_out"))
        z_banked, abs_done, ln_done, sp_done, acc_banked, t_done, a_done, sb_pv = (
            sem(n) for n in ("z_banked", "abs_done", "ln_done", "sp_done", "acc_banked", "t_done", "a_done",
                             "sb_pv"))
        sb_out = sem("sb_out")
        logits_banked, shifted, exp_logits, sel_done, pos_banked, count_done, moe_done = (
            sem(n) for n in ("logits_banked", "shifted", "exp_logits", "sel_done", "pos_banked", "count_done",
                             "moe_done"))
        prep_done, gather_banked, gather_hi, gathered, pgt_banked, pgt_done, e_silu, e_prod, h_banked, \
            hT_done, hT_lo_done, y_done, sc_banked, sc_done = (
                sem("e_" + n) for n in ("prep", "gather_banked", "gather_hi", "gathered", "pgt_banked",
                                        "pgt_done", "silu", "prod", "h_banked", "hT", "hT_lo", "y",
                                        "sc_banked", "sc_done"))

        posm = rt[:, 0:16].rearrange("p (e t) -> p e t", t=TB)
        gate = rt[:, 16:32].rearrange("p (e t) -> p e t", t=TB)

        class Steps:

            def __init__(self, sem, eng=None):
                self.sem, self.n, self.eng = sem, 0, eng

            def __call__(self, ins):
                self.n += 1
                ins.then_inc(self.sem, 1)

            def settle(self):
                self.eng.wait_ge(self.sem, self.n)

        vs, as_ = Steps(dve_step), Steps(act_step)

        def f32(ap):
            return ap.bitcast(F32)

        def bc(ap, n, at=1):
            shape = list(ap.shape)
            shape.insert(at, n)
            return ap.unsqueeze(at).to_broadcast(shape)

        def mm3(out_, a_hi, a_lo, b_hi, b_lo, first, last, **kw):
            nc.tensor.matmul(out_, a_hi, b_hi, start=first, stop=False, **kw)
            nc.tensor.matmul(out_, a_hi, b_lo, start=False, stop=False, **kw)
            return nc.tensor.matmul(out_, a_lo, b_hi, start=False, stop=last, **kw)

        def hi_unit(act, src, buf, width, full, unit):
            act.wait_ge(*full)
            act.wait_ge(unit_used, unit + 1)
            nc.scalar.activation(w_hi[:, buf, 0:width], src, ACT.Copy).then_inc(hi_ready, 1)

        def lo_unit(dve, src, buf, width, unit):
            dve.wait_ge(hi_ready, unit + 1)
            nc.vector.tensor_tensor(w_lo[:, buf, 0:width], src, f32(w_hi[:, buf, 0:width]),
                                    ALU.subtract).then_inc(split_ready, 1)

        class InProj:

            def __init__(self, layer, w, cols, dst, unit0, loads0):
                self.layer, self.cols, self.dst, self.unit0 = layer, cols, dst, unit0
                self.width = cols // IN_CH
                self.w = w[0].rearrange("(h k p) (i n) -> p h k i n", p=P, k=4, n=2 * self.width)
                self.loads0 = loads0

            def view(self, ap):
                return ap[:, 0:4 * self.width]

            def hi(self, act, i, jj):
                for u in range(4):
                    s = 2 * jj + u // 2
                    src = ring[s][:, (u % 2) * 2 * self.width:(u % 2 + 1) * 2 * self.width]
                    hi_unit(act, src, u, 2 * self.width,
                            (slot_full[s], 16 * (self.loads0 + i + 1)), self.unit0 + 8 * i + 4 * jj + u)

            def evac(self, act, i, jj):
                act.wait_ge(unit_used, self.unit0 + 8 * i + 4 * jj + 4 + NBUF)
                for tb in range(TB):
                    ins = nc.scalar.activation(
                        self.dst[:, tb, bass.ds(i * (2 * self.width) + jj * self.width, self.width)],
                        pb[2 * jj + tb][:, 0:self.width], ACT.Copy)
                ins.then_inc(proj_done, 1)

            def act(self, act):
                self.hi(act, 0, 0)
                with act.Fori(0, IN_CH // 2 - 1) as i:
                    self.hi(act, i, 1)
                    self.evac(act, i, 0)
                    self.hi(act, i + 1, 0)
                    self.evac(act, i, 1)
                n = IN_CH // 2 - 1
                self.hi(act, n, 1)
                self.evac(act, n, 0)
                self.evac(act, n, 1)

            def dve(self, dve):
                with dve.Fori(0, IN_CH // 2) as i:
                    for jj in range(2):
                        for u in range(4):
                            s = 2 * jj + u // 2
                            src = ring[s][:, (u % 2) * 2 * self.width:(u % 2 + 1) * 2 * self.width]
                            lo_unit(dve, src, u, 2 * self.width, self.unit0 + 8 * i + 4 * jj + u)

            def pe(self, pe):
                w = self.width
                with pe.Fori(0, IN_CH // 2) as i:
                    for jj in range(2):
                        pe.wait_ge(proj_done, IN_CH * self.layer + 2 * i + jj + 1)
                        for u in range(4):
                            pe.wait_ge(split_ready, self.unit0 + 8 * i + 4 * jj + u + 1)
                            for kk in range(2):
                                k = 2 * u + kk
                                for tb in range(TB):
                                    t = slice(tb * P, tb * P + P)
                                    ins = mm3(pb[2 * jj + tb][:, 0:w], xT_hi[:, k, t], xT_lo[:, k, t],
                                              w_hi[:, u, kk * w:kk * w + w], w_lo[:, u, kk * w:kk * w + w],
                                              k == 0, k == KD - 1)
                            ins.then_inc(unit_used, 1)

            def load(self, sp, i, jj, half):
                dst = ring[2 * jj + half][:, 0:4 * self.width].rearrange("p (k n) -> p k n", k=4)
                src = self.w[:, half, :, bass.ds(i, 1), jj * self.width:(jj + 1) * self.width].rearrange(
                    "p k a n -> p (k a) n")
                sp.dma_start(dst, src).then_inc(slot_full[2 * jj + half], 16)

            def loads_rest(self, sp):
                with sp.Fori(1, IN_CH // 2) as i:
                    for jj in range(2):
                        for half in range(2):
                            sp.wait_ge(split_ready, self.unit0 + 8 * i - 8 + 4 * jj + 2 * half + 2)
                            self.load(sp, i, jj, half)

        ab = InProj(0, ab_w_in, AB_IN, proj, U_AB_IN, 0)
        cd = InProj(1, cd_w_in, CD_IN, proj1, U_CD_IN, 12)

        def norm_act(act, use, gain, dst):
            if use:
                act.wait_ge(h_done, 4 * use)
            else:
                act.wait_ge(x_in, 16)
                act.wait_ge(consts_in, 16)
            for tb in range(TB):
                nc.scalar.activation(xn[:, tb, :], h[:, tb, :], ACT.Square,
                                     accum_out=ss[:, tb:tb + 1]).then_inc(sq_done, 1)
            act.wait_ge(sq_done, 2 * use + 2)
            nc.scalar.activation(rms, ss, ACT.Sqrt, bias=const("eps"), scale=1.0 / D).then_inc(rms_done, 1)
            for k in range(KD):
                act.wait_ge(xT_banked, 4 * use + k // 2 + 1)
                nc.scalar.activation(dst[:, k, :], pb[k // 2][:, (k % 2) * 256:(k % 2) * 256 + 256], ACT.Copy,
                                     scale=const(gain, k, k + 1)).then_inc(xT_hi_done, 1)

        def norm_dve(dve, use, gain, split=True):
            dve.wait_ge(rms_done, use + 1)
            nc.vector.reciprocal(rstd, rms).then_inc(rstd_done, 1)
            dve.wait_ge(rstd_done, use + 1)
            for tb in range(TB):
                nc.vector.tensor_scalar(xn[:, tb, :], h[:, tb, :], rstd[:, tb:tb + 1], None,
                                        ALU.mult).then_inc(xn_done, 1)
            if split:
                for k in range(KD):
                    dve.wait_ge(xT_hi_done, KD * use + (k // 2) * 2 + 2)
                    nc.vector.scalar_tensor_tensor(
                        out=xT_lo[:, k, :], in0=pb[k // 2][:, (k % 2) * 256:(k % 2) * 256 + 256],
                        scalar=const(gain, k, k + 1), in1=f32(xT_hi[:, k, :]), op0=ALU.mult,
                        op1=ALU.subtract).then_inc(xT_done, 1)

        def norm_pe(pe, use):
            pe.wait_ge(xn_done, 2 * use + 2)
            for b in range(4):
                for kk in range(2):
                    for tb in range(TB):
                        k = 2 * b + kk
                        ins = nc.tensor.transpose(pb[b][:, kk * 256 + tb * P:kk * 256 + tb * P + P],
                                                  xn[:, tb, k * P:k * P + P], const("ident"))
                ins.then_inc(xT_banked, 1)

        def mix_pe(pe, layer, src):
            pe.wait_ge(mix_done, layer + 1)
            for b in range(6):
                if layer and b == 4:
                    pe.wait_ge(sb_out, 2)
                for kk in range(2):
                    for tb in range(TB):
                        k = 2 * b + kk
                        ins = nc.tensor.transpose(pb[b][:, kk * 256 + tb * P:kk * 256 + tb * P + P],
                                                  src[:, tb, k * P:k * P + P], const("ident"))
                ins.then_inc(mixT_banked, 1)
            pe.wait_ge(mixT_done, KM * layer + KM)
            unit0 = U_CD_OUT if layer else U_AB_OUT
            for k in range(KM):
                pe.wait_ge(split_ready, unit0 + k + 1)
                for tb in range(TB):
                    for n in range(2):
                        t = slice(tb * P, tb * P + P)
                        w = slice(n * 512, n * 512 + 512)
                        ins = mm3(pb[2 * tb + n], mixT_hi[:, k, t], mixT_lo[:, k, t],
                                  w_hi[:, k % NBUF, w], w_lo[:, k % NBUF, w], k == 0, k == KM - 1)
                ins.then_inc(unit_used, 1)

        OUT_SLOTS = {0: [0, 1, 2, 3, 4, 5], 1: [4, 5, 6, 0, 1, 2]}
        OUT_BEFORE = {0: [4, 4, 4, 4, 1, 1], 1: [9, 9, 1, 16, 16, 16]}

        def mix_act(act, layer, gain):
            for k in range(KM):
                act.wait_ge(mixT_banked, 6 * layer + k // 2 + 1)
                nc.scalar.activation(mixT_hi[:, k, :], pb[k // 2][:, (k % 2) * 256:(k % 2) * 256 + 256], ACT.Copy,
                                     scale=const(gain, k, k + 1)).then_inc(mixT_hi_done, 1)
            unit0 = U_CD_OUT if layer else U_AB_OUT
            for k in range(KM):
                s, before = OUT_SLOTS[layer][k // 2], OUT_BEFORE[layer][k // 2]
                hi_unit(act, ring[s][:, (k % 2) * UNIT:(k % 2 + 1) * UNIT], k % NBUF, UNIT,
                        (slot_full[s], 16 * (before + 1)), unit0 + k)

        def mix_dve(dve, layer, gain):
            for k in range(KM):
                dve.wait_ge(mixT_hi_done, KM * layer + (k // 2) * 2 + 2)
                nc.vector.scalar_tensor_tensor(
                    out=mixT_lo[:, k, :], in0=pb[k // 2][:, (k % 2) * 256:(k % 2) * 256 + 256],
                    scalar=const(gain, k, k + 1), in1=f32(mixT_hi[:, k, :]), op0=ALU.mult,
                    op1=ALU.subtract).then_inc(mixT_done, 1)
            unit0 = U_CD_OUT if layer else U_AB_OUT
            for k in range(KM):
                s = OUT_SLOTS[layer][k // 2]
                lo_unit(dve, ring[s][:, (k % 2) * UNIT:(k % 2 + 1) * UNIT], k % NBUF, UNIT, unit0 + k)
            dve.wait_ge(unit_used, unit0 + KM + NBUF)
            for tb in range(TB):
                for n in range(2):
                    w = slice(n * 512, n * 512 + 512)
                    nc.vector.tensor_tensor(h[:, tb, w], h[:, tb, w], pb[2 * tb + n], ALU.add).then_inc(h_done, 1)

        class Softmax:

            def __init__(self, heads, first, q, k, v, bias, coef, sinks, turn_banks, out_at):
                self.turn_banks = turn_banks
                self.heads, self.first, self.q, self.k, self.v = heads, first, q, k, v
                self.bias, self.coef, self.sinks, self.out_at = bias, coef, sinks, out_at

            def scores(self, pe, i):
                n = self.first + i
                if n >= 2:
                    pe.wait_ge(nm_done, n - 1)
                q, k = self.q(i), self.k(i)
                nc.tensor.matmul(pb[i % 2][:, 0:P], q[:, 0:P], k[:, 0:P], start=True, stop=True)
                nc.tensor.matmul(pb[i % 2][:, P:384], q[:, P:256], k[:, 0:256], start=True,
                                 stop=True).then_inc(s_banked, 1)

            def turn(self, pe, i):
                n = self.first + i
                pe.wait_ge(exp_done, 2 * n + 2)
                if n >= len(self.turn_banks):
                    pe.wait_ge(pT_done, n + 1 - len(self.turn_banks))
                for b in range(3):
                    ins = nc.tensor.transpose(pb[self.turn_banks[i % len(self.turn_banks)]][:, b * P:b * P + P],
                                              p_sb[i % 2][:, b * P:b * P + P], const("ident"))
                ins.then_inc(pT_banked, 1)

            def values(self, pe, i):
                pe.wait_ge(pT_done, self.first + i + 1)
                pT, (o0, o1) = pT_sb[i % 2], self.out_at(i)
                nc.tensor.matmul(o0, pT[:, 0:P], self.v(i, 0), start=True, stop=True)
                nc.tensor.matmul(o1, pT[:, P:2 * P], self.v(i, 0), start=True, stop=False)
                nc.tensor.matmul(o1, pT[:, 2 * P:384], self.v(i, 1), start=False,
                                 stop=True).then_inc(pv_done, 1)

            def pe_step(self, pe, i):
                if i < self.heads:
                    self.scores(pe, i)
                if 1 <= i <= self.heads:
                    self.turn(pe, i - 1)
                if 2 <= i < self.heads + 2:
                    self.values(pe, i - 2)

            def dve_step(self, dve, i):
                if i >= self.heads:
                    return
                n = self.first + i
                dve.wait_ge(s_banked, n + 1)
                if n >= 2:
                    dve.wait_ge(exp_done, 2 * n - 2)
                vs(nc.vector.scalar_tensor_tensor(out=s_sb[i % 2], in0=self.bias, scalar=self.coef(i),
                                                  in1=pb[i % 2][:, 0:384], op0=ALU.mult, op1=ALU.add))
                vs.settle()
                vs(nc.vector.tensor_reduce(mx[:, 2 * i:2 * i + 1], s_sb[i % 2][:, 0:P], AX, ALU.max))
                vs(nc.vector.tensor_reduce(mx[:, 2 * i + 1:2 * i + 2], s_sb[i % 2][:, P:384], AX, ALU.max))
                vs.settle()
                m = mx[:, 2 * i:2 * i + 2]
                if self.sinks is None:
                    ins = nc.vector.tensor_scalar(nm[:, 2 * i:2 * i + 2], m, -1.0, None, ALU.mult)
                else:
                    ins = nc.vector.tensor_scalar(nm[:, 2 * i:2 * i + 2], m, self.sinks[:, i:i + 1], -1.0,
                                                  ALU.max, ALU.mult)
                ins.then_inc(nm_done, 1)

            def act_step(self, act, i):
                if i < self.heads:
                    n = self.first + i
                    act.wait_ge(nm_done, n + 1)
                    if n >= 2:
                        act.wait_ge(pT_banked, n - 1)
                    for t, (a, b) in enumerate(((0, P), (P, 384))):
                        nc.scalar.activation(p_sb[i % 2][:, a:b], s_sb[i % 2][:, a:b], ACT.Exp,
                                             bias=nm[:, 2 * i + t:2 * i + t + 1],
                                             accum_out=sm[:, 2 * i + t:2 * i + t + 1]).then_inc(exp_done, 1)
                if 1 <= i <= self.heads:
                    n = self.first + i - 1
                    act.wait_ge(pT_banked, n + 1)
                    if n >= 2:
                        act.wait_ge(pv_done, n - 1)
                    bank = pb[self.turn_banks[(i - 1) % len(self.turn_banks)]]
                    nc.scalar.activation(pT_sb[(i - 1) % 2], bank[:, 0:384], ACT.Copy).then_inc(pT_done, 1)

        def quad_at(bank, i):
            return tuple(bank[:, tb * 256 + (i % 4) * 64:tb * 256 + (i % 4) * 64 + 64] for tb in range(TB))

        def half_rows(i):
            return slice((i % 2) * 64, (i % 2) * 64 + 64)

        mla = Softmax(MLA_H, 0, lambda i: qT[0:MLA_D, i, :], lambda i: kT[0:MLA_D, i, :],
                      lambda i, t: kvh[:, t, i * 128 + NOPE:i * 128 + 128], const("causal"), lambda i: 1.0, None, (2, 7),
                      lambda i: (pb[3][:, i * 64:i * 64 + 64], pb[4][:, i * 64:i * 64 + 64]))
        swa = Softmax(SWA_H, MLA_H, lambda i: cT[half_rows(i), i // 2, :],
                      lambda i: cT[half_rows(i), 8 + i // 8, :],
                      lambda i, t: proj1[:, t, C_SV + (i // 8) * 64:C_SV + (i // 8) * 64 + 64], const("dist"),
                      lambda i: -2.0 ** (-8.0 * (i + 1) / SWA_H), const("sinks"), (2,),
                      lambda i: quad_at(pb[3 + i // 4 % 2], i))

        def l0_act(act):
            act.wait_ge(proj_done, IN_CH + 2)
            for tb in range(TB):
                as_(nc.scalar.activation(mix[:, tb, 0:Q_RANK], proj[:, tb, 0:Q_RANK], ACT.Square,
                                         accum_out=ss4[:, tb:tb + 1]))
                as_(nc.scalar.activation(mix[:, tb, Q_RANK:A_KR], proj[:, tb, A_KV:A_KR], ACT.Square,
                                         accum_out=ss4[:, 2 + tb:3 + tb]))
            as_.settle()
            nc.scalar.activation(rs4[:, 0:2], ss4[:, 0:2], ACT.Sqrt, bias=const("eps"),
                                 scale=1.0 / Q_RANK).then_inc(lat_rms, 1)
            nc.scalar.activation(rs4[:, 2:4], ss4[:, 2:4], ACT.Sqrt, bias=const("eps"),
                                 scale=1.0 / KV_RANK).then_inc(lat_rms, 1)
            for tb in range(TB):
                nc.scalar.activation(proj[:, tb, A_RG:AB_IN], proj[:, tb, A_RG:AB_IN],
                                     ACT.Silu).then_inc(silu_rg, 1)
            act.wait_ge(qkv_banked, 1)
            for nh in range(2):
                for tb in range(TB):
                    ins = nc.scalar.activation(qh[:, tb, nh * 384:nh * 384 + 384],
                                               pb[3 + 2 * nh + tb][:, 0:384], ACT.Copy)
            ins.then_inc(qh_done, 1)
            act.wait_ge(qkv_banked, 2)
            for nh in range(2):
                for tb in range(TB):
                    ins = nc.scalar.activation(kvh[:, tb, nh * 512:nh * 512 + 512],
                                               pb[(7, 0, 1, 2)[2 * nh + tb]], ACT.Copy)
            ins.then_inc(kvh_done, 1)
            act.wait_ge(kvh_done, 1)
            for tb in range(TB):
                ins = nc.scalar.activation(
                    kcat[:, tb, :].rearrange("p (h d) -> p h d", d=MLA_D)[:, :, 0:NOPE],
                    kvh[:, tb, :].rearrange("p (h d) -> p h d", d=128)[:, :, 0:NOPE], ACT.Copy)
            ins.then_inc(nope_done, 1)
            act.wait_ge(q_banked, 1)
            for b in range(4):
                ins = nc.scalar.activation(qT[0:MLA_D, 2 * b:2 * b + 2, :].rearrange("p h t -> p (h t)"),
                                           pb[3 + b][0:MLA_D, :], ACT.Copy, scale=MLA_D ** -0.5)
            ins.then_inc(qT_done, 1)
            act.wait_ge(r_banked, 1)
            for b in range(4):
                ins = nc.scalar.activation(rT[:, 2 * b:2 * b + 2, :].rearrange("p h t -> p (h t)"),
                                           pb[3 + b], ACT.Copy)
            ins.then_inc(rT_done, 1)
            for i in range(MLA_H + 1):
                mla.act_step(act, i)
            act.wait_ge(gn_var, 1)
            nc.scalar.activation(gn_t[:, 128:144],
                                 gn_t[:, 96:128].rearrange("p (g s) -> p g s", s=2)[:, :, 1], ACT.Sqrt,
                                 bias=const("eps")).then_inc(gn_sd, 1)

        def rope(x_, cos, sin, half, a, b, out_, heads=None):
            vs(nc.vector.tensor_tensor(a, x_, cos, ALU.mult))
            vs(nc.vector.tensor_tensor(b[:, :, 0:half], x_[:, :, half:2 * half], sin[:, :, 0:half], ALU.mult))
            vs(nc.vector.tensor_tensor(b[:, :, half:2 * half], x_[:, :, 0:half], sin[:, :, half:2 * half],
                                       ALU.mult))
            vs.settle()
            if heads is not None:
                a, b = (t[:, 0, :].unsqueeze(1).to_broadcast([P, heads, 2 * half]) for t in (a, b))
            return nc.vector.tensor_tensor(out_, a, b, ALU.add)

        def l0_dve(dve):
            dve.wait_ge(lat_rms, 2)
            vs(nc.vector.reciprocal(ri4, rs4))
            vs.settle()
            for tb in range(TB):
                nc.vector.tensor_scalar(proj[:, tb, 0:Q_RANK], proj[:, tb, 0:Q_RANK], ri4[:, tb:tb + 1], None,
                                        ALU.mult).then_inc(lat_scaled, 1)
                nc.vector.tensor_scalar(proj[:, tb, A_KV:A_KR], proj[:, tb, A_KV:A_KR], ri4[:, 2 + tb:3 + tb],
                                        None, ALU.mult).then_inc(lat_scaled, 1)
            dve.wait_ge(unit_used, U_AB_OUT + NBUF)
            t3 = rope_t.rearrange("p (a n) -> p a n", n=32)

            def rot_r(tb):
                ins = rope(proj[:, tb, A_RQK:A_RV].rearrange("p (h d) -> p h d", d=64),
                           bc(const("cos_r", 64 * tb, 64 * tb + 64), 16), bc(const("sin_r", 64 * tb, 64 * tb + 64), 16),
                           32, rqk[:, tb, :].rearrange("p (h d) -> p h d", d=64),
                           rope_t.rearrange("p (h d) -> p h d", d=64),
                           rqk[:, tb, :].rearrange("p (h d) -> p h d", d=64))
                ins.then_inc(rqk_done, 1)
                dve.wait_ge(rqk_done, tb + 1)

            for tb in range(TB):
                ins = rope(proj[:, tb, A_KR:A_RQK].unsqueeze(1), bc(const("cos_m", 32 * tb, 32 * tb + 32), 1),
                           bc(const("sin_m", 32 * tb, 32 * tb + 32), 1), 16, t3[:, 2 * tb:2 * tb + 1, :],
                           t3[:, 2 * tb + 1:2 * tb + 2, :],
                           kcat[:, tb, :].rearrange("p (h d) -> p h d", d=MLA_D)[:, :, NOPE:MLA_D], heads=MLA_H)
                ins.then_inc(kcat_done, 1)
                dve.wait_ge(kcat_done, tb + 1)
            dve.wait_ge(lat_banked, 1)
            for b in range(5):
                ins = nc.vector.tensor_scalar(latT[:, b, :], pb[b // 2][:, (b % 2) * 256:(b % 2) * 256 + 256],
                                              const("g_lat", b, b + 1), None, ALU.mult)
            ins.then_inc(latT_done, 1)
            rot_r(0)
            dve.wait_ge(qh_done, 1)
            for tb in range(TB):
                xq = qh[:, tb, :].rearrange("p (h d) -> p h d", d=MLA_D)[:, :, NOPE:MLA_D]
                ins = rope(xq, bc(const("cos_m", 32 * tb, 32 * tb + 32), 8),
                           bc(const("sin_m", 32 * tb, 32 * tb + 32), 8), 16, t3[:, 0:8, :], t3[:, 8:16, :], xq)
                ins.then_inc(qrope_done, 1)
                dve.wait_ge(qrope_done, tb + 1)
            rot_r(1)
            dve.wait_ge(k_banked, 1)
            for b in range(4):
                ins = nc.vector.tensor_copy(kT[0:MLA_D, 2 * b:2 * b + 2, :].rearrange("p h t -> p (h t)"),
                                            pb[(7, 0, 1, 2)[b]][0:MLA_D, :])
            ins.then_inc(kT_done, 1)
            for i in range(MLA_H + 0):
                mla.dve_step(dve, i)
            dve.wait_ge(pv_done, MLA_H)
            vs(nc.vector.reciprocal(rsm[:, 0:2 * MLA_H], sm[:, 0:2 * MLA_H]))
            vs.settle()
            r2 = rsm[:, 0:2 * MLA_H].rearrange("p (h t) -> p h t", t=TB)
            for tb in range(TB):
                nc.vector.tensor_tensor(mix[:, tb, 0:512].rearrange("p (h d) -> p h d", d=64),
                                        pb[3 + tb].rearrange("p (h d) -> p h d", d=64),
                                        bc(r2[:, :, tb], 64, 2), ALU.mult).then_inc(mla_out, 1)
            dve.wait_ge(decay_in, 16)
            for i in range(RET_H):
                dve.wait_ge(ret_banked, i + 1)
                if i >= 2:
                    dve.wait_ge(ret_out, i - 1)
                nc.vector.tensor_tensor(s_sb[i % 2][:, 0:256], pb[i % 2][:, 0:256], decay[:, i, :],
                                        ALU.mult).then_inc(ret_decayed, 1)
                nc.vector.tensor_tensor(s_sb[i % 2][:, 256:384], pb[i % 2][:, 256:384], decay[:, i, 0:P],
                                        ALU.mult).then_inc(ret_decayed, 1)
            dve.wait_ge(ret_out, RET_H)
            groups = [(tb, i) for tb in range(TB) for i in range(RET_H)]

            def ret_o(tb, i):
                return pb[3 + 2 * tb + i // 4][:, (i % 4) * P:(i % 4) * P + P]

            for g, (tb, i) in enumerate(groups):
                vs(nc.vector.bn_stats(gn_t[:, 6 * g:6 * g + 6], ret_o(tb, i)))
            vs.settle()
            for g in range(len(groups)):
                ins = nc.vector.bn_aggr(gn_t[:, 96 + 2 * g:98 + 2 * g], gn_t[:, 6 * g:6 * g + 6])
                ins.then_inc(*((gn_var, 1) if g == len(groups) - 1 else (dve_step, 1)))
                vs.n += g != len(groups) - 1
            dve.wait_ge(gn_sd, 1)
            vs(nc.vector.reciprocal(gn_t[:, 144:160], gn_t[:, 128:144]))
            vs.settle()
            for g, (tb, i) in enumerate(groups):
                vs(nc.vector.tensor_scalar(mix[:, tb, 512 + i * P:512 + i * P + P], ret_o(tb, i),
                                           gn_t[:, 96 + 2 * g:97 + 2 * g], gn_t[:, 144 + g:145 + g],
                                           ALU.subtract, ALU.mult))
            vs.settle()
            for tb in range(TB):
                ins = nc.vector.tensor_tensor(mix[:, tb, 512:MIX], mix[:, tb, 512:MIX], proj[:, tb, A_RG:AB_IN],
                                              ALU.mult)
            ins.then_inc(mix_done, 1)

        def l0_pe(pe):
            pe.wait_ge(lat_scaled, 4)
            for b in range(5):
                c0 = b * P
                for tb in range(TB):
                    ins = nc.tensor.transpose(pb[b // 2][:, (b % 2) * 256 + tb * P:(b % 2) * 256 + tb * P + P],
                                              proj[:, tb, c0:c0 + P], const("ident"))
            ins.then_inc(lat_banked, 1)
            pe.wait_ge(latT_done, 1)
            for nh in range(2):
                pe.wait_ge(slot_full[4 + nh], 16)
                for tb in range(TB):
                    for k in range(3):
                        ins = nc.tensor.matmul(pb[3 + 2 * nh + tb][:, 0:384], latT[:, k, tb * P:tb * P + P],
                                               ring[4 + nh][:, k * 384:k * 384 + 384], start=k == 0, stop=k == 2)
            ins.then_inc(qkv_banked, 1)
            pe.wait_ge(slot_full[6], 16)
            for nh in range(2):
                for tb in range(TB):
                    for k in range(2):
                        ins = nc.tensor.matmul(pb[(7, 0, 1, 2)[2 * nh + tb]], latT[:, 3 + k, tb * P:tb * P + P],
                                               ring[6][:, k * 1024 + nh * 512:k * 1024 + nh * 512 + 512],
                                               start=k == 0, stop=k == 1)
            ins.then_inc(qkv_banked, 1)
            pe.wait_ge(qrope_done, 2)
            for i in range(MLA_H):
                for tb in range(TB):
                    c0 = (i % 2) * 256 + tb * P
                    ins = nc.tensor.transpose(pb[3 + i // 2][0:MLA_D, c0:c0 + P],
                                              qh[:, tb, i * MLA_D:i * MLA_D + MLA_D], const("ident"))
            ins.then_inc(q_banked, 1)
            pe.wait_ge(nope_done, 1)
            pe.wait_ge(kcat_done, 2)
            for i in range(MLA_H):
                for tb in range(TB):
                    c0 = (i % 2) * 256 + tb * P
                    ins = nc.tensor.transpose(pb[(7, 0, 1, 2)[i // 2]][0:MLA_D, c0:c0 + P],
                                              kcat[:, tb, i * MLA_D:i * MLA_D + MLA_D], const("ident"))
            ins.then_inc(k_banked, 1)
            pe.wait_ge(qT_done, 1)
            pe.wait_ge(rqk_done, 2)
            for b in range(8):
                for tb in range(TB):
                    c0 = (b % 2) * 256 + tb * P
                    ins = nc.tensor.transpose(pb[3 + b // 2][:, c0:c0 + P], rqk[:, tb, b * P:b * P + P],
                                              const("ident"))
            ins.then_inc(r_banked, 1)
            pe.wait_ge(kT_done, 1)
            pe.wait_ge(rT_done, 1)
            for i in range(MLA_H + 2):
                mla.pe_step(pe, i)

            def ret_values(i):
                pe.wait_ge(ret_decayed, 2 * i + 2)
                o0, o1 = (pb[3 + 2 * tb + i // 4][:, (i % 4) * P:(i % 4) * P + P] for tb in range(TB))
                v0, v1 = (proj[:, tb, A_RV + i * P:A_RV + i * P + P] for tb in range(TB))
                a = s_sb[i % 2]
                nc.tensor.matmul(o0, a[:, 0:P], v0, start=True, stop=True)
                nc.tensor.matmul(o1, a[:, P:256], v0, start=True, stop=False)
                nc.tensor.matmul(o1, a[:, 256:384], v1, start=False, stop=True).then_inc(ret_out, 1)

            for i in range(RET_H + 1):
                if i < RET_H:
                    if i >= 2:
                        pe.wait_ge(ret_decayed, 2 * i - 2)
                    r = half_rows(i)
                    nc.tensor.matmul(pb[i % 2][:, 0:256], rT[r, 4 + i // 2, 0:P], rT[r, i // 2, :],
                                     start=True, stop=True)
                    nc.tensor.matmul(pb[i % 2][:, 256:384], rT[r, 4 + i // 2, P:256], rT[r, i // 2, P:256],
                                     start=True, stop=True).then_inc(ret_banked, 1)
                if i == 1:
                    pe.wait_ge(mla_out, 2)
                if i >= 1:
                    ret_values(i - 1)

        Z_BANKS = (6, 7)
        L1_STEPS = 2 * SB_H + 4

        def l1_act(act):
            for r in range(0, 9, 2):
                act.wait_ge(cT_banked, r + 1)
                nc.scalar.activation(cT[:, 2 * r:2 * r + 2, :].rearrange("p b t -> p (b t)"), pb[r % 8], ACT.Copy,
                                     scale=0.125 if r in (0, 2, 6) else 1.0).then_inc(cT_act, 1)

            def ln_part(i):
                b = sb_buf[0][i % 3]
                act.wait_ge(abs_done, i + 1)
                as_(nc.scalar.activation(b, b, ACT.Exp))
                as_.settle()
                nc.scalar.activation(b, b, ACT.Ln, bias=1.0).then_inc(ln_done, 1)

            def weights(i):
                act.wait_ge(t_done, i + 1)
                if i >= 3:
                    act.wait_ge(sb_pv, i - 2)
                nc.scalar.activation(sb_buf[3][i % 3], sb_buf[2][i % 3], ACT.Exp).then_inc(a_done, 1)

            def quad_out(bank, m, col, done):
                nc.scalar.activation(mix1[:, :, col + 256 * m:col + 256 * m + 256],
                                     bank.rearrange("p (b c) -> p b c", b=TB), ACT.Copy).then_inc(done, 1)

            for i in range(L1_STEPS + 1):
                swa.act_step(act, i)
                if i == SWA_H + 1:
                    act.wait_ge(sink_in, 1)
                    nc.scalar.activation(snk, snk, ACT.Exp).then_inc(sink_exp, 1)
                if i % 2 and i < 2 * SB_H:
                    ln_part(i // 2)
                if i % 2 == 0 and 4 <= i < 2 * SB_H + 4:
                    weights((i - 4) // 2)
                if i % 4 == 2 and 6 <= i <= SWA_H + 2:
                    m = (i - 6) // 4
                    act.wait_ge(pv_done, MLA_H + 4 * m + 4)
                    quad_out(pb[3 + m % 2], m, 0, swa_out)
                if i % 8 == 4 and i > 4:
                    m = i // 8 - 1
                    act.wait_ge(sb_pv, 4 * m + 4)
                    quad_out(pb[5], m, SWA_H * HD, sb_out)

        def l1_dve(dve):
            dve.wait_ge(proj_done, 2 * IN_CH + 2)
            for tb in range(TB):
                nc.vector.tensor_copy(
                    kdup[:, tb, :].rearrange("p (g r d) -> p g r d", g=2, r=2),
                    bc(proj1[:, tb, C_SK:C_SV].rearrange("p (g d) -> p g d", d=HD), 2, 2)).then_inc(kdup_done, 1)
            for r in range(1, 9, 2):
                dve.wait_ge(cT_banked, r + 1)
                o = cT[:, 2 * r:2 * r + 2, :].rearrange("p b t -> p (b t)")
                if r == 7:
                    ins = nc.vector.tensor_copy(o, pb[r])
                else:
                    ins = nc.vector.tensor_scalar(o, pb[r], 0.125, None, ALU.mult)
                ins.then_inc(cT_dve, 1)

            def minus_abs(i):
                dve.wait_ge(z_banked, i + 1)
                z = pb[Z_BANKS[i % 2]][:, 0:384]
                if i >= 3:
                    dve.wait_ge(a_done, i - 2)
                    dve.wait_ge(sp_done, i - 2)
                vs(nc.vector.tensor_scalar(sb_buf[2][i % 3], z, -1.0, None, ALU.mult))
                vs.settle()
                nc.vector.tensor_tensor(sb_buf[0][i % 3], sb_buf[2][i % 3], z, ALU.min).then_inc(abs_done, 1)

            def softplus(i):
                dve.wait_ge(ln_done, i + 1)
                if i >= 3:
                    dve.wait_ge(acc_banked, i - 2)
                z, sp_ = pb[Z_BANKS[i % 2]][:, 0:384], sb_buf[1][i % 3]
                vs(nc.vector.scalar_tensor_tensor(out=sp_, in0=z, scalar=0.0, in1=sb_buf[0][i % 3], op0=ALU.max,
                                                  op1=ALU.add))
                vs.settle()
                v = sp_.rearrange("p (b q) -> p b q", q=P)[:, 0:3:2, :]
                nc.vector.tensor_tensor(v, v, bc(const("before"), 2), ALU.mult).then_inc(sp_done, 1)

            def masked(i):
                dve.wait_ge(acc_banked, i + 1)
                nc.vector.tensor_tensor(sb_buf[2][i % 3], pb[Z_BANKS[i % 2]][:, 0:384], const("sb_neg"),
                                        ALU.add).then_inc(t_done, 1)

            n2 = 2 * SWA_H
            for i in range(2 * SB_H + 2):
                if i % 2 and i < 2 * SB_H:
                    minus_abs(i // 2)
                swa.dve_step(dve, i)
                if i % 2 == 0 and i:
                    softplus(i // 2 - 1)
                if i % 2 and i >= 3:
                    masked((i - 3) // 2)
                if i == SWA_H:
                    dve.wait_ge(nm_done, MLA_H + SWA_H)
                    nc.vector.tensor_tensor(snk[:, 0:n2].rearrange("p (h t) -> p h t", t=TB),
                                            bc(const("sinks"), TB, 2),
                                            nm[:, 0:n2].rearrange("p (h t) -> p h t", t=TB),
                                            ALU.add).then_inc(sink_in, 1)
            dve.wait_ge(sink_exp, 1)
            vs(nc.vector.tensor_tensor(sm[:, 0:n2], sm[:, 0:n2], snk[:, 0:n2], ALU.add))
            vs.settle()
            vs(nc.vector.reciprocal(rsm[:, 0:n2], sm[:, 0:n2]))
            dve.wait_ge(swa_out, 4)
            vs.settle()
            r2 = rsm[:, 0:n2].rearrange("p (h t) -> p h t", t=TB)
            for tb in range(TB):
                o = mix1[:, tb, 0:SWA_H * HD].rearrange("p (h d) -> p h d", d=HD)
                ins = nc.vector.tensor_tensor(o, o, bc(r2[:, :, tb], HD, 2), ALU.mult)
            ins.then_inc(mix_done, 1)

        def l1_pe(pe):
            pe.wait_ge(proj_done, 2 * IN_CH + 2)
            pe.wait_ge(kdup_done, 2)
            for r in range(9):
                if r == 8:
                    pe.wait_ge(cT_act, 1)
                for kk in range(2):
                    b = 2 * r + kk
                    for tb in range(TB):
                        if b < 8:
                            src = proj1[:, tb, b * P:b * P + P]
                        elif b < 10:
                            src = kdup[:, tb, (b - 8) * P:(b - 8) * P + P]
                        else:
                            src = proj1[:, tb, C_BQ + (b - 10) * P:C_BQ + (b - 10) * P + P]
                        ins = nc.tensor.transpose(pb[r % 8][:, kk * 256 + tb * P:kk * 256 + tb * P + P], src,
                                                  const("ident"))
                ins.then_inc(cT_banked, 1)
            pe.wait_ge(cT_act, 5)
            pe.wait_ge(cT_dve, 4)

            def z_scores(i):
                if i >= 2:
                    pe.wait_ge(t_done, i - 1)
                r, z = half_rows(i), pb[Z_BANKS[i % 2]]
                q, k = cT[r, 10 + i // 2, :], cT[r, 14 + i // 2, :]
                nc.tensor.matmul(z[:, 0:256], k[:, 0:P], q[:, 0:256], start=True, stop=False,
                                 skip_group_check=True)
                nc.tensor.matmul(z[:, 256:384], k[:, P:256], q[:, P:256], start=False, stop=False,
                                 skip_group_check=True).then_inc(z_banked, 1)

            def log_after(i):
                pe.wait_ge(sp_done, i + 1)
                z, sp_ = pb[Z_BANKS[i % 2]], sb_buf[1][i % 3]
                nc.tensor.matmul(z[:, 0:256], const("incl"), sp_[:, 0:256], start=False, stop=False,
                                 skip_group_check=True)
                nc.tensor.matmul(z[:, P:256], const("negones"), sp_[:, 256:384], start=False, stop=False,
                                 skip_group_check=True)
                nc.tensor.matmul(z[:, 256:384], const("incl"), sp_[:, 256:384], start=False, stop=True,
                                 skip_group_check=True).then_inc(acc_banked, 1)

            def weigh(i):
                pe.wait_ge(a_done, i + 1)
                if i == 4:
                    pe.wait_ge(sb_out, 1)
                a, (o0, o1) = sb_buf[3][i % 3], quad_at(pb[5], i)
                v0, v1 = (proj1[:, tb, C_BV + i * 64:C_BV + i * 64 + 64] for tb in range(TB))
                nc.tensor.matmul(o0, a[:, 0:P], v0, start=True, stop=True)
                nc.tensor.matmul(o1, a[:, P:256], v0, start=True, stop=False)
                nc.tensor.matmul(o1, a[:, 256:384], v1, start=False, stop=True).then_inc(sb_pv, 1)

            for i in range(L1_STEPS):
                if i % 4 == 2 and 10 <= i < SWA_H + 2:
                    pe.wait_ge(swa_out, i // 4 - 1)
                swa.pe_step(pe, i)
                if i % 2 and 3 <= i < 2 * SB_H + 3:
                    log_after((i - 3) // 2)
                if i % 2 and i >= 5:
                    weigh((i - 5) // 2)
                if i % 2 == 0 and i < 2 * SB_H:
                    z_scores(i // 2)

        def f_unit(kind, c):
            if kind == "d":
                return U_FFN + 8 + 12 * c + 4
            return U_FFN + 8 + 12 * (c - 1) + (0 if kind == "g" else 8)

        F_SLOT = dict(g=0, u=2, d=4)
        F_BEFORE = dict(g=5, u=5, d=2)

        def f_src(kind, half, u):
            return ring[F_SLOT[kind] + half][:, u * UNIT:u * UNIT + UNIT]

        def f_load(sp, kind, c, half):
            s = F_SLOT[kind] + half
            if kind == "d":
                dst = ring[s].rearrange("p (k n) -> p k n", k=2)
                src = f_down[0, bass.ds(c * FC + half * 256, 256), :].rearrange("(k p) n -> p k n", p=P)
            else:
                dst = ring[s].rearrange("p (k n) -> p k n", k=4)
                w = f_gate if kind == "g" else f_up
                src = w[0, half * 512:half * 512 + 512, bass.ds(c * FC, FC)].rearrange("(k p) n -> p k n", p=P)
            sp.dma_start(dst, src).then_inc(slot_full[s], 16)

        def f_hi(act, kind, c, first):
            for u in range(4):
                s = F_SLOT[kind] + u // 2
                hi_unit(act, f_src(kind, u // 2, u % 2), u, UNIT, (slot_full[s], 16 * (F_BEFORE[kind] + c + 1)),
                        first + u)

        def f_lo(dve, kind, first):
            for u in range(4):
                lo_unit(dve, f_src(kind, u // 2, u % 2), u, UNIT, first + u)

        def f_gate_up(pe, kind, c, first):
            b0 = 0 if kind == "g" else 2
            for u in range(4):
                pe.wait_ge(split_ready, first + u + 1)
                for kk in range(2):
                    k = 2 * u + kk
                    for j in range(4):
                        w = slice(kk * 512 + j * P, kk * 512 + j * P + P)
                        ins = mm3(pb[b0 + j // 2][:, (j % 2) * 256:(j % 2) * 256 + 256], w_hi[:, u, w],
                                  w_lo[:, u, w], xT_hi[:, k, :], xT_lo[:, k, :], k == 0 and j % 2 == 0,
                                  k == KD - 1, skip_group_check=True)
                ins.then_inc(unit_used, 1)

        def f_down_pe(pe, first, start, stop):
            for t in range(4):
                pe.wait_ge(split_ready, first + t + 1)
                for tb in range(TB):
                    for n in range(2):
                        w, tk = slice(n * 512, n * 512 + 512), slice(tb * P, tb * P + P)
                        ins = mm3(pb[4 + 2 * tb + n], fT_hi[:, t, tk], fT_lo[:, t, tk], w_hi[:, t, w],
                                  w_lo[:, t, w], start and t == 0, stop and t == 3, skip_group_check=True)
                ins.then_inc(unit_used, 1)

        def f_silu_act(act, c, g_end):
            act.wait_ge(unit_used, g_end + NBUF)
            act.wait_ge(f_lo_done, 2 * c + 2)
            for b in range(2):
                nc.scalar.activation(fg[:, 2 * b:2 * b + 2, :].rearrange("p j t -> p (j t)"), pb[b],
                                     ACT.Silu).then_inc(f_silu, 1)

        def f_round(act, c):
            act.wait_ge(f_prod, 2 * c + 2)
            nc.scalar.activation(fT_hi, fg, ACT.Copy).then_inc(f_hi_done, 1)

        def f_prod_dve(dve, c, u_end):
            dve.wait_ge(unit_used, u_end + NBUF)
            for b in range(2):
                dve.wait_ge(f_silu, 2 * c + b + 1)
                v = fg[:, 2 * b:2 * b + 2, :].rearrange("p j t -> p (j t)")
                nc.vector.tensor_tensor(v, v, pb[2 + b], ALU.mult).then_inc(f_prod, 1)

        def f_rest(dve, c):
            dve.wait_ge(f_hi_done, c + 1)
            nc.vector.tensor_tensor(fT_lo, fg, f32(fT_hi), ALU.subtract).then_inc(f_lo_done, 2)

        def ffn_act(act):
            f_hi(act, "g", 0, U_FFN)
            f_hi(act, "u", 0, U_FFN + 4)
            f_silu_act(act, 0, U_FFN + 4)
            with act.Fori(1, NFC) as c:
                f_hi(act, "g", c, f_unit("g", c))
                f_round(act, c - 1)
                f_hi(act, "d", c - 1, f_unit("d", c - 1))
                f_silu_act(act, c, f_unit("g", c) + 4)
                f_hi(act, "u", c, f_unit("u", c))
            f_round(act, NFC - 1)
            f_hi(act, "d", NFC - 1, U_FFN + 8 + 12 * (NFC - 1))

        def ffn_dve(dve):
            f_lo(dve, "g", U_FFN)
            f_lo(dve, "u", U_FFN + 4)
            with dve.Fori(1, NFC) as c:
                f_lo(dve, "g", f_unit("g", c))
                f_prod_dve(dve, c - 1, f_unit("g", c))
                f_rest(dve, c - 1)
                f_lo(dve, "d", f_unit("d", c - 1))
                f_lo(dve, "u", f_unit("u", c))
            f_prod_dve(dve, NFC - 1, U_FFN + 8 + 12 * (NFC - 1))
            f_rest(dve, NFC - 1)
            f_lo(dve, "d", U_FFN + 8 + 12 * (NFC - 1))
            dve.wait_ge(unit_used, U_CD_IN + NBUF)
            for tb in range(TB):
                for n in range(2):
                    w = slice(n * 512, n * 512 + 512)
                    nc.vector.tensor_tensor(h[:, tb, w], h[:, tb, w], pb[4 + 2 * tb + n], ALU.add).then_inc(h_done, 1)

        def ffn_pe(pe):
            pe.wait_ge(xT_done, 2 * KD)
            f_gate_up(pe, "g", 0, U_FFN)
            f_gate_up(pe, "u", 0, U_FFN + 4)

            def middle(c, start):
                pe.wait_ge(f_silu, 2 * c)
                f_gate_up(pe, "g", c, f_unit("g", c))
                pe.wait_ge(f_lo_done, 2 * c + 2)
                f_down_pe(pe, f_unit("d", c - 1), start, False)
                f_gate_up(pe, "u", c, f_unit("u", c))

            middle(1, True)
            with pe.Fori(2, NFC) as c:
                middle(c, False)
            pe.wait_ge(f_lo_done, 2 * NFC + 2)
            f_down_pe(pe, U_FFN + 8 + 12 * (NFC - 1), False, True)

        items = moe_items()
        plan = [(kind, c, half) for kind, c in items for half in range(2)]
        UPE = 2 * len(plan)
        SC_BANKS = (6, 7, 2, 3)
        m_slot = [(m + 7) % MOE_SLOTS for m in range(len(plan))]
        M_BEFORE = [17, 17, 17, 16, 10, 10, 2] + [0] * 7

        def m_loaded(m, q):
            s = m_slot[m]
            return slot_full[s], 16 * (3 * q + (M_BEFORE[s] + m // MOE_SLOTS + 1))

        def m_done(m, q):
            return split_ready, UPE * q + (U_MOE + 2 * m + 2)

        def m_used(kind, c, q):
            return unit_used, UPE * q + (U_MOE + 4 * items.index((kind, c)) + 4 + NBUF)

        def m_load(sp, m, e):
            kind, c, half = plan[m]
            s = m_slot[m]
            if kind == "d":
                dst = ring[s].rearrange("p (k n) -> p k n", k=2)
                src = m_down[0, bass.ds(e, 1), c * FC + half * 256:c * FC + half * 256 + 256, :].rearrange(
                    "e (k p) n -> p (e k) n", p=P)
            else:
                dst = ring[s].rearrange("p (k n) -> p k n", k=4)
                w = m_gate if kind == "g" else m_up
                src = w[0, bass.ds(e, 1), half * 512:half * 512 + 512, c * FC:c * FC + FC].rearrange(
                    "e (k p) n -> p (e k) n", p=P)
            sp.dma_start(dst, src).then_inc(slot_full[s], 16)

        def m_loads(sp, lo, hi, e, q):
            for m in range(lo, hi):
                if m < MOE_SLOTS:
                    sp.wait_ge(*m_done(m - MOE_SLOTS + len(plan), q - 1))
                else:
                    sp.wait_ge(*m_done(m - MOE_SLOTS, q))
                m_load(sp, m, e)

        def moe_sp(sp, part):
            n, q0 = len(plan), NE * part
            if part:
                m_loads(sp, 0, MOE_SLOTS, 0, q0)
            with sp.Fori(0, NE - 1) as e:
                m_loads(sp, MOE_SLOTS, n, e, e + q0)
                m_loads(sp, 0, MOE_SLOTS, e + 1, e + (q0 + 1))
            m_loads(sp, MOE_SLOTS, n, NE - 1, q0 + NE - 1)

        def m_src(m, u):
            return ring[m_slot[m]][:, u * UNIT:u * UNIT + UNIT]

        def m_units(item):
            n0 = 4 * items.index(item)
            return [(n // 2, n % 2, n, n % NBUF) for n in range(n0, n0 + 4)]

        def m_hi(act, item, q, units=slice(0, 4)):
            for m, u, n, buf in m_units(item)[units]:
                hi_unit(act, m_src(m, u), buf, UNIT, m_loaded(m, q), UPE * q + (U_MOE + n))

        def m_lo(dve, item, q, units=slice(0, 4)):
            for m, u, n, buf in m_units(item)[units]:
                lo_unit(dve, m_src(m, u), buf, UNIT, UPE * q + (U_MOE + n))

        def gather_act(act, r, q):
            act.wait_ge(gather_banked, 2 * q + (r + 1))
            nc.scalar.activation(xe_hi[:, 4 * r:4 * r + 4, :].rearrange("p k t -> p (k t)"), pb[2 + r],
                                 ACT.Copy).then_inc(gather_hi, 1)

        def gather_dve(dve, r, q):
            dve.wait_ge(gather_hi, 2 * q + (r + 1))
            nc.vector.tensor_tensor(xe_lo[:, 4 * r:4 * r + 4, :].rearrange("p k t -> p (k t)"), pb[2 + r],
                                    f32(xe_hi[:, 4 * r:4 * r + 4, :].rearrange("p k t -> p (k t)")),
                                    ALU.subtract).then_inc(gathered, 1)

        def gather_pe(pe, r):
            for kk in range(4):
                k = 4 * r + kk
                for tb in range(TB):
                    ins = nc.tensor.matmul(pb[2 + r][:, kk * P:kk * P + P], xn[:, tb, k * P:k * P + P],
                                           pick[:, tb, :], start=tb == 0, stop=tb == 1)
            ins.then_inc(gather_banked, 1)

        def prepare(dve, e, part):
            for tb in range(TB):
                e_ = slice(e, e + 1) if isinstance(e, int) else bass.ds(e, 1)
                place_of = posm[:, e_, tb]
                places = const("iota", CAP * part, CAP * part + CAP)
                nc.vector.tensor_scalar(pick[:, tb, :], places, place_of, None, ALU.is_equal).then_inc(prep_done, 1)
                nc.vector.tensor_scalar(pick_g[:, tb, :], places, place_of, gate[:, e_, tb], ALU.is_equal,
                                        ALU.mult).then_inc(prep_done, 1)

        LAST = NFC - 1

        def moe_act(act, part):
            def silu_(c, q):
                act.wait_ge(*m_used("g", c, q))
                act.wait_ge(h_banked, 7 * q + max(c, 1))
                nc.scalar.activation(eh[c % 2], pb[2 * (c % 2)], ACT.Silu).then_inc(e_silu, 1)

            def turned(c, q):
                act.wait_ge(h_banked, 7 * q + (c + 2))
                nc.scalar.activation(hT_hi.rearrange("p j t -> p (j t)"), pb[6], ACT.Copy).then_inc(hT_done, 1)

            def outputs(q):
                act.wait_ge(*m_used("d", LAST, q))
                act.wait_ge(sc_done, 4 * q + 4)
                for n in range(2):
                    ins = nc.scalar.activation(y_sb[:, n * 512:n * 512 + 512], pb[4 + n], ACT.Copy)
                ins.then_inc(y_done, 1)

            def expert(e, q, last):
                for c in range(1, NFC):
                    m_hi(act, ("g", c), q)
                    m_hi(act, ("u", c), q)
                    turned(c - 1, q)
                    if c == 1:
                        act.wait_ge(pgt_banked, q + 1)
                        nc.scalar.activation(pick_gT.rearrange("p b t -> p (b t)"), pb[7][:, 0:256],
                                             ACT.Copy).then_inc(pgt_done, 1)
                    silu_(c, q)
                    m_hi(act, ("d", c - 1), q)
                m_hi(act, ("d", LAST), q, slice(0, 3))
                turned(LAST, q)
                m_hi(act, ("d", LAST), q, slice(3, 4))
                if last:
                    outputs(q)
                    return
                for r in range(2):
                    gather_act(act, r, q + 1)
                m_hi(act, ("g", 0), q + 1, slice(0, 3))
                outputs(q)
                m_hi(act, ("g", 0), q + 1, slice(3, 4))
                m_hi(act, ("u", 0), q + 1)
                silu_(0, q + 1)

            q0 = NE * part
            for r in range(2):
                gather_act(act, r, q0)
            m_hi(act, ("g", 0), q0)
            m_hi(act, ("u", 0), q0)
            silu_(0, q0)
            with act.Fori(0, NE - 1) as e:
                expert(e, e + q0, False)
            expert(NE - 1, q0 + NE - 1, True)

        def moe_dve(dve, part):
            def product(c, q):
                dve.wait_ge(*m_used("u", c, q))
                dve.wait_ge(e_silu, 7 * q + (c + 1))
                nc.vector.tensor_tensor(eh[c % 2], eh[c % 2], pb[2 * (c % 2) + 1], ALU.mult).then_inc(e_prod, 1)

            def rest(c, q):
                dve.wait_ge(hT_done, 7 * q + (c + 1))
                nc.vector.tensor_tensor(hT_lo.rearrange("p j t -> p (j t)"), pb[6],
                                        f32(hT_hi.rearrange("p j t -> p (j t)")),
                                        ALU.subtract).then_inc(hT_lo_done, 1)

            def add(q):
                for s in range(4):
                    tb, w = s // 2, slice((s % 2) * 512, (s % 2) * 512 + 512)
                    dve.wait_ge(sc_banked, 4 * q + (s + 1))
                    nc.vector.tensor_tensor(h[:, tb, w], h[:, tb, w], pb[SC_BANKS[s]], ALU.add).then_inc(sc_done, 1)

            def expert(e, q, last):
                for c in range(1, NFC):
                    m_lo(dve, ("g", c), q)
                    if c == 1:
                        product(0, q)
                    m_lo(dve, ("u", c), q)
                    rest(c - 1, q)
                    if c < LAST:
                        m_lo(dve, ("d", c - 1), q)
                        product(c, q)
                    if c == 1 and not last:
                        dve.wait_ge(pgt_banked, q + 1)
                        prepare(dve, e + 1, part)
                m_lo(dve, ("d", LAST - 1), q, slice(0, 3))
                product(LAST, q)
                m_lo(dve, ("d", LAST - 1), q, slice(3, 4))
                m_lo(dve, ("d", LAST), q, slice(0, 3))
                rest(LAST, q)
                m_lo(dve, ("d", LAST), q, slice(3, 4))
                if not last:
                    for r in range(2):
                        gather_dve(dve, r, q + 1)
                    m_lo(dve, ("g", 0), q + 1)
                    m_lo(dve, ("u", 0), q + 1)
                add(q)

            q0 = NE * part
            prepare(dve, 0, part)
            for r in range(2):
                gather_dve(dve, r, q0)
            m_lo(dve, ("g", 0), q0)
            m_lo(dve, ("u", 0), q0)
            with dve.Fori(0, NE - 1) as e:
                expert(e, e + q0, False)
            expert(NE - 1, q0 + NE - 1, True)
            dve.wait_ge(sc_done, 4 * (q0 + NE) + 4)

        def moe_pe(pe, part):
            def gate_up(kind, c, q):
                bank = pb[2 * (c % 2) + (kind == "u")]
                for m, u, n, buf in m_units((kind, c)):
                    pe.wait_ge(split_ready, UPE * q + (U_MOE + n + 1))
                    for kk in range(2):
                        k = 4 * plan[m][2] + 2 * u + kk
                        w = slice(kk * 512, kk * 512 + 512)
                        ins = mm3(bank, xe_hi[:, k, :], xe_lo[:, k, :], w_hi[:, buf, w], w_lo[:, buf, w],
                                  k == 0, k == KD - 1)
                    ins.then_inc(unit_used, 1)

            def turn(c, q):
                pe.wait_ge(e_prod, 7 * q + (c + 2))
                if c:
                    pe.wait_ge(hT_lo_done, 7 * q + c)
                for j in range(4):
                    ins = nc.tensor.transpose(pb[6][:, j * P:j * P + P], eh[c % 2][:, j * P:j * P + P],
                                              const("ident"))
                ins.then_inc(h_banked, 1)

            def down(c, q):
                pe.wait_ge(hT_lo_done, 7 * q + (c + 1))
                if c == 0:
                    pe.wait_ge(y_done, q + 1)
                for m, u, n, buf in m_units(("d", c)):
                    t = 2 * plan[m][2] + u
                    pe.wait_ge(split_ready, UPE * q + (U_MOE + n + 1))
                    for nn in range(2):
                        w = slice(nn * 512, nn * 512 + 512)
                        ins = mm3(pb[4 + nn], hT_hi[:, t, :], hT_lo[:, t, :], w_hi[:, buf, w],
                                  w_lo[:, buf, w], c == 0 and t == 0, c == LAST and t == 3)
                    ins.then_inc(unit_used, 1)

            def scatter(q):
                pe.wait_ge(y_done, q + 2)
                for s in range(4):
                    nc.tensor.matmul(pb[SC_BANKS[s]], pick_gT[:, s // 2, :],
                                     y_sb[:, (s % 2) * 512:(s % 2) * 512 + 512], start=True,
                                     stop=True).then_inc(sc_banked, 1)

            def expert(q, last):
                for c in range(1, NFC):
                    if c == 1:
                        pe.wait_ge(sc_done, 4 * q + 4)
                    pe.wait_ge(e_prod, 7 * q + c)
                    gate_up("g", c, q)
                    turn(c - 1, q)
                    if c == 1:
                        for tb in range(TB):
                            ins = nc.tensor.transpose(pb[7][:, tb * P:tb * P + P], pick_g[:, tb, :],
                                                      const("ident"))
                        ins.then_inc(pgt_banked, 1)
                    gate_up("u", c, q)
                    down(c - 1, q)
                turn(LAST, q)
                if last:
                    down(LAST, q)
                    scatter(q)
                    return
                pe.wait_ge(prep_done, 4 * q + 8)
                for r in range(2):
                    gather_pe(pe, r)
                down(LAST, q)
                first(q + 1)
                scatter(q)
                gate_up("u", 0, q + 1)

            def first(q):
                pe.wait_ge(gathered, 2 * q + 2)
                pe.wait_ge(e_prod, 7 * q + 1)
                gate_up("g", 0, q)

            q0 = NE * part
            pe.wait_ge(rows_scaled, TB)
            pe.wait_ge(prep_done, 4 * q0 + 4)
            pe.wait_ge(sc_done, 4 * q0 + 4)
            for r in range(2):
                gather_pe(pe, r)
            first(q0)
            gate_up("u", 0, q0)
            with pe.Fori(0, NE - 1) as e:
                expert(e + q0, False)
            expert(q0 + NE - 1, True)

        lg, gt, eq, rank, sel = (rt[:, a:b] for a, b in ((36, 52), (64, 192), (192, 320), (320, 336), (336, 352)))
        lmax, shf, ex, num, den, rden, cmax, pos1 = (
            rt[:, a:b] for a, b in ((352, 354), (356, 372), (372, 388), (388, 404), (404, 406), (406, 408),
                                    (408, 409), (412, 428)))

        def route_pe(pe):
            pe.wait_ge(router_in, 16)
            pe.wait_ge(xT_hi_done, 4 * KD)
            for tb in range(TB):
                for k in range(KD):
                    ins = nc.tensor.matmul(pb[4][:, tb * NE:tb * NE + NE], xT32[:, k, tb * P:tb * P + P],
                                           router_sb[:, k, :], start=k == 0, stop=k == KD - 1)
            ins.then_inc(logits_banked, 1)
            pe.wait_ge(sel_done, 1)
            s0, s1 = sel[:, 0:NE], sel[:, NE:2 * NE]
            nc.tensor.matmul(pb[5][:, 0:8], const("strict"), s0, start=True, stop=True)
            nc.tensor.matmul(pb[5][:, 8:16], const("ones"), s0, start=True, stop=False)
            nc.tensor.matmul(pb[5][:, 8:16], const("strict"), s1, start=False, stop=True)
            nc.tensor.matmul(pb[5][:, 16:24], const("ones"), s0, start=True, stop=False)
            nc.tensor.matmul(pb[5][:, 16:24], const("ones"), s1, start=False, stop=True).then_inc(pos_banked, 1)

        def route_act(act):
            act.wait_ge(shifted, 2)
            nc.scalar.activation(ex, shf, ACT.Exp).then_inc(exp_logits, 1)

        def route_dve(dve):
            dve.wait_ge(logits_banked, 1)
            vs(nc.vector.tensor_copy(lg, pb[4][:, 0:16]))
            vs.settle()
            for tb in range(TB):
                l = lg[:, tb * NE:tb * NE + NE]
                g3 = gt[:, 64 * tb:64 * tb + 64].rearrange("p (j i) -> p j i", i=NE)
                e3 = eq[:, 64 * tb:64 * tb + 64].rearrange("p (j i) -> p j i", i=NE)
                vs(nc.vector.tensor_tensor(g3, bc(l, NE, 1), bc(l, NE, 2), ALU.is_gt))
                vs(nc.vector.tensor_tensor(e3, bc(l, NE, 1), bc(l, NE, 2), ALU.is_equal))
            vs(nc.vector.tensor_reduce(lmax, lg.rearrange("p (t e) -> p t e", e=NE), AX, ALU.max))
            vs.settle()
            for tb in range(TB):
                e2 = eq[:, 64 * tb:64 * tb + 64]
                vs(nc.vector.tensor_tensor(e2, e2, const("lower8"), ALU.mult))
                nc.vector.tensor_scalar(shf[:, tb * NE:tb * NE + NE], lg[:, tb * NE:tb * NE + NE],
                                        lmax[:, tb:tb + 1], None, ALU.subtract).then_inc(shifted, 1)
            vs.settle()
            vs(nc.vector.tensor_tensor(gt, gt, eq, ALU.add))
            vs.settle()
            vs(nc.vector.tensor_reduce(rank, gt.rearrange("p (j i) -> p j i", i=NE), AX, ALU.add))
            vs.settle()
            nc.vector.tensor_scalar(sel, rank, 2.0, None, ALU.is_lt).then_inc(sel_done, 1)
            dve.wait_ge(g_moe_in, 16)
            for tb in range(TB):
                nc.vector.tensor_tensor(xn[:, tb, :], xn[:, tb, :], g_moe_row, ALU.mult).then_inc(rows_scaled, 1)
            dve.wait_ge(sel_done, 1)
            dve.wait_ge(exp_logits, 1)
            vs(nc.vector.tensor_tensor(num, ex, sel, ALU.mult))
            vs.settle()
            vs(nc.vector.tensor_reduce(den, num.rearrange("p (t e) -> p t e", e=NE), AX, ALU.add))
            vs.settle()
            vs(nc.vector.reciprocal(rden, den))
            dve.wait_ge(pos_banked, 1)
            vs(nc.vector.tensor_reduce(cmax, pb[5][:, 16:24], AX, ALU.max))
            vs(nc.vector.scalar_tensor_tensor(out=pos1, in0=pb[5][:, 0:16], scalar=1.0, in1=sel, op0=ALU.add,
                                              op1=ALU.mult))
            vs.settle()
            for tb in range(TB):
                vs(nc.vector.tensor_scalar(gate[:, 0:NE, tb], num[:, tb * NE:tb * NE + NE], rden[:, tb:tb + 1],
                                           None, ALU.mult))
                vs(nc.vector.tensor_scalar(posm[:, 0:NE, tb], pos1[:, tb * NE:tb * NE + NE], -1.0, None, ALU.add))
            vs.settle()
            nc.vector.tensor_copy(cnt_i[:, 0:1], cmax).then_inc(count_done, 1)

        def overflow(eng, body):
            eng.wait_ge(count_done, 1)
            most = eng.value_load(cnt_i[0:1, 0:1], min_val=0, max_val=256)
            with eng.If(most > CAP):
                body(eng, 1)

        block = ctx.enter_context(nc.Block())

        @block.sync
        def _(sp):
            sp.dma_start(h, x[0].rearrange("(b p) d -> p b d", p=P)).then_inc(x_in, 16)
            sp.dma_start(cst, consts).then_inc(consts_in, 16)
            for jj in range(2):
                for half in range(2):
                    ab.load(sp, 0, jj, half)
            for nh in range(2):
                sp.dma_start(ring[4 + nh][:, 0:1152].rearrange("p (k n) -> p k n", k=3),
                             w_uq[0].rearrange("(k p) n -> p k n", p=P)[:, :, nh * 384:nh * 384 + 384]).then_inc(
                                 slot_full[4 + nh], 16)
            sp.dma_start(ring[6].rearrange("p (k n) -> p k n", k=2),
                         w_ukv[0].rearrange("(k p) n -> p k n", p=P)).then_inc(slot_full[6], 16)
            sp.dma_start(router_sb, router[0].rearrange("(k p) e -> p k e", p=P)).then_inc(router_in, 16)
            ab.loads_rest(sp)

            def out_load(w, layer, i):
                s = OUT_SLOTS[layer][i]
                sp.dma_start(ring[s].rearrange("p (k n) -> p k n", k=2),
                             w[0, 256 * i:256 * i + 256, :].rearrange("(k p) n -> p k n", p=P)).then_inc(
                                 slot_full[s], 16)

            for i in range(4):
                sp.wait_ge(split_ready, U_AB_IN + 24 + 2 * i + 2)
                out_load(ab_w_out, 0, i)
            sp.wait_ge(unit_used, U_AB_OUT + NBUF)
            sp.dma_start(decay, decay_t).then_inc(decay_in, 16)
            sp.wait_ge(qkv_banked, 1)
            for i in range(4, 6):
                out_load(ab_w_out, 0, i)
            for kind, i0 in (("g", 0), ("u", 2)):
                for half in range(2):
                    sp.wait_ge(split_ready, U_AB_OUT + 2 * (i0 + half) + 2)
                    f_load(sp, kind, 0, half)
            for kind in "gdu":
                for half in range(2):
                    done = {"g": U_FFN, "d": U_AB_OUT + 8, "u": U_FFN + 4}[kind] + 2 * half + 2
                    sp.wait_ge(split_ready, done)
                    f_load(sp, kind, 0 if kind == "d" else 1, half)
            with sp.Fori(2, NFC) as c:
                for kind in "gdu":
                    cc = c - 1 if kind == "d" else c
                    for half in range(2):
                        sp.wait_ge(split_ready, f_unit(kind, cc - 1) + (2 * half + 2))
                        f_load(sp, kind, cc, half)
            for half in range(2):
                sp.wait_ge(split_ready, f_unit("d", NFC - 2) + 2 * half + 2)
                f_load(sp, "d", NFC - 1, half)
            for jj, kind in enumerate("gu"):
                for half in range(2):
                    sp.wait_ge(split_ready, f_unit(kind, NFC - 1) + 2 * half + 2)
                    cd.load(sp, 0, jj, half)
            cd.loads_rest(sp)
            d6 = U_FFN + 8 + 12 * (NFC - 1)
            for i, done in enumerate((d6 + 2, d6 + 4, None, U_CD_IN + 26, U_CD_IN + 28, U_CD_IN + 30)):
                if done is None:
                    sp.wait_ge(qkv_banked, 2)
                else:
                    sp.wait_ge(split_ready, done)
                out_load(cd_w_out, 1, i)
            sp.wait_ge(mixT_done, 2 * KM)
            sp.dma_start(g_moe_row, moe_gain).then_inc(g_moe_in, 16)
            sp.dma_start(fgain, final_gain).then_inc(gain_in, 16)
            for m in range(MOE_SLOTS):
                s = m_slot[m]
                if s < 7:
                    last = {4: 2, 5: 4, 6: 6, 0: 8, 1: 10, 2: 12}.get(s, 0)
                    sp.wait_ge(split_ready, U_CD_OUT + last)
                m_load(sp, m, 0)
            moe_sp(sp, 0)
            overflow(sp, moe_sp)
            sp.wait_ge(xn_done, 10)
            sp.dma_start(out[0].rearrange("(b p) d -> p b d", p=P), xn).then_inc(out_done, 16)
            sp.wait_ge(out_done, 16)

        @block.scalar
        def _(act):
            as_.eng = act
            norm_act(act, 0, "g_ab", xT_hi)
            ab.act(act)
            l0_act(act)
            mix_act(act, 0, "g_mix")
            norm_act(act, 1, "g_ffn", xT_hi)
            ffn_act(act)
            norm_act(act, 2, "g_cd", xT_hi)
            cd.act(act)
            l1_act(act)
            mix_act(act, 1, "g_one")
            norm_act(act, 3, "g_moe", xT32)
            route_act(act)
            moe_act(act, 0)
            overflow(act, moe_act)
            act.wait_ge(moe_done, 1)
            for tb in range(TB):
                nc.scalar.activation(xn[:, tb, :], h[:, tb, :], ACT.Square,
                                     accum_out=ss[:, tb:tb + 1]).then_inc(sq_done, 1)
            act.wait_ge(sq_done, 10)
            nc.scalar.activation(rms, ss, ACT.Sqrt, bias=const("eps"), scale=1.0 / D).then_inc(rms_done, 1)

        @block.tensor
        def _(pe):
            pe.sem_inc(unit_used, NBUF)
            pe.sem_inc(h_banked, 1)
            norm_pe(pe, 0)
            pe.wait_ge(xT_done, KD)
            ab.pe(pe)
            l0_pe(pe)
            mix_pe(pe, 0, mix)
            norm_pe(pe, 1)
            ffn_pe(pe)
            norm_pe(pe, 2)
            pe.wait_ge(xT_done, 3 * KD)
            cd.pe(pe)
            l1_pe(pe)
            mix_pe(pe, 1, mix1)
            norm_pe(pe, 3)
            route_pe(pe)
            moe_pe(pe, 0)
            overflow(pe, moe_pe)

        @block.vector
        def _(dve):
            vs.eng = dve
            dve.sem_inc(f_lo_done, 2)
            dve.sem_inc(e_prod, 1)
            dve.sem_inc(sc_done, 4)
            dve.sem_inc(y_done, 1)
            dve.sem_inc(proj_done, 2)
            dve.wait_ge(x_in, 16)
            dve.wait_ge(consts_in, 16)
            norm_dve(dve, 0, "g_ab")
            ab.dve(dve)
            l0_dve(dve)
            mix_dve(dve, 0, "g_mix")
            norm_dve(dve, 1, "g_ffn")
            ffn_dve(dve)
            norm_dve(dve, 2, "g_cd")
            cd.dve(dve)
            l1_dve(dve)
            mix_dve(dve, 1, "g_one")
            norm_dve(dve, 3, "g_moe", split=False)
            route_dve(dve)
            moe_dve(dve, 0)
            overflow(dve, moe_dve)
            dve.wait_ge(gain_in, 16)
            dve.sem_inc(moe_done, 1)
            dve.wait_ge(rms_done, 5)
            nc.vector.reciprocal(rstd, rms).then_inc(rstd_done, 1)
            dve.wait_ge(rstd_done, 5)
            for tb in range(TB):
                nc.vector.scalar_tensor_tensor(out=xn[:, tb, :], in0=h[:, tb, :], scalar=rstd[:, tb:tb + 1],
                                               in1=fgain, op0=ALU.mult, op1=ALU.mult).then_inc(xn_done, 1)


def shape_tables(np):
    i = np.arange(P)
    row, col = i[:, None], i[None, :]
    f = np.float32
    t = {}
    t["ident"] = (row == col).astype(f)
    t["incl"] = -(row >= col).astype(f)
    t["negones"] = -np.ones((P, P), f)
    t["ones"] = np.ones((P, P), f)
    t["before"] = (row < col).astype(f)
    t["strict"] = (row < col).astype(f)
    t["iota"] = np.broadcast_to(np.arange(256, dtype=f), (P, 256))

    def rotary(half):
        inv = (10000.0 ** (-np.arange(half, dtype=f) / half)).astype(f)
        ang = (np.arange(256, dtype=f)[:, None] * inv[None, :]).astype(np.float64)
        c, s = np.cos(ang).astype(f), np.sin(ang).astype(f)
        c, s = np.concatenate([c, c], 1), np.concatenate([-s, s], 1)
        return [m.reshape(2, P, 2 * half).transpose(1, 0, 2).reshape(P, 4 * half) for m in (c, s)]

    t["cos_m"], t["sin_m"] = rotary(16)
    t["cos_r"], t["sin_r"] = rotary(32)
    diag = np.where(col > row, f(MASKED), f(0))
    zero = np.zeros((P, P), f)
    t["causal"] = np.concatenate([diag, zero, diag], 1)
    d0 = np.where(col > row, f(-MASKED), (row - col).astype(f))
    d1 = np.where(col > row, (row + P - col).astype(f), f(-MASKED))
    t["dist"] = np.concatenate([d0, d1, d0], 1)
    neg = np.where(row >= col, f(MASKED), f(0))
    t["sb_neg"] = np.concatenate([neg, zero, neg], 1)
    e = np.arange(8)
    t["lower8"] = np.broadcast_to((e[None, :] < e[:, None]).astype(f).reshape(1, 64), (P, 64))
    t["g_one"] = np.ones((P, KM), f)
    t["eps"] = np.full((P, 1), EPS, f)
    lg = np.log1p(-(2.0 ** (-5.0 - np.arange(RET_H))))
    rel = np.arange(256)[None, None, :] - i[:, None, None]
    decay = np.where(rel >= 0, np.exp(lg[None, :, None] * np.maximum(rel, 0)), 0.0) * RET_DK ** -0.5
    return t, decay.astype(f)


def kernel(**inputs):
    import numpy as np
    import concourse.bacc as bacc
    from concourse.bass_utils import run_bass_kernel_spmd as run

    a = {k: np.asarray(v) for k, v in inputs.items()}
    t, decay = shape_tables(np)

    def columns(g):
        return g.reshape(-1, P).T

    t["g_ab"], t["g_ffn"] = columns(a["ab_norm"][0]), columns(a["ffn_norm"][0])
    t["g_cd"], t["g_moe"] = columns(a["cd_norm"][0]), columns(a["moe_norm"][0])
    t["g_lat"] = np.concatenate([columns(a["mla_q_norm"][0]), columns(a["mla_kv_norm"][0])], 1)
    t["g_mix"] = np.concatenate([np.ones((P, 4), np.float32), columns(a["ret_gn"][0])], 1)
    t["sinks"] = np.broadcast_to(a["swa_sinks"][0][None, :], (P, SWA_H))
    consts = np.ascontiguousarray(np.concatenate([t[n] for n in CONST_WIDTHS], 1))
    assert consts.shape == (P, NCONST) and consts.dtype == np.float32

    nc = bacc.Bacc("TRN2", target_bir_lowering=False, num_devices=1)
    given = dict(x=a["x"], consts=consts, decay=decay, ab_w_in=a["ab_w_in"], w_uq=a["mla_w_uq"],
                 w_ukv=a["mla_w_ukv"], ab_w_out=a["ab_w_out"], f_gate=a["ffn_w_gate"], f_up=a["ffn_w_up"],
                 f_down=a["ffn_w_down"], cd_w_in=a["cd_w_in"], cd_w_out=a["cd_w_out"], router=a["moe_router"],
                 m_gate=a["moe_w_gate"], m_up=a["moe_w_up"], m_down=a["moe_w_down"],
                 moe_gain=np.broadcast_to(a["moe_norm"][0][None, :], (P, D)),
                 final_gain=np.broadcast_to(a["final_norm"][None, :], (P, D)))
    arrays, aps = {}, []
    for name, v in given.items():
        arrays[name + "_dram"] = v = np.ascontiguousarray(v)
        aps.append(nc.dram_tensor(name + "_dram", v.shape, mybir.dt.from_np(v.dtype), kind="ExternalInput").ap())
    out = nc.dram_tensor("out_dram", (1, 256, D), F32, kind="ExternalOutput").ap()
    trunk(nc, *aps, out)
    r = run(nc, [arrays], core_ids=[0])
    return r.results[0]["out_dram"]
```
